# Optimizing a Trainium2 kernel written in Bass

```python
import jax, jax.numpy as jnp
from jax import lax
import numpy as np
import math

D_MODEL = 1024
BATCH = 1
SEQ = 512
DEPTH = 2

N_MIXERS = 2
N_LRU = (DEPTH + 1) // 2
N_FOX = DEPTH // 2
D_RNN = D_MODEL
LRU_BLOCKS = 16
LRU_BLOCK_DIM = D_RNN // LRU_BLOCKS
CONV_WIDTH = 4
LRU_C = 8.0
N_HEADS = 16
HEAD_DIM = D_MODEL // N_HEADS
Q_BLOCK = 128
D_FF = 4 * D_MODEL
EPS = 1e-6
NEG_INF = -1e30


def rms_norm(x, g):
    xf = x.astype(jnp.float32)
    y = xf * lax.rsqrt(jnp.mean(xf * xf, axis=-1, keepdims=True) + EPS)
    return (y * g.astype(jnp.float32)).astype(x.dtype)

def causal_depthwise_conv(x, w, b):
    S = x.shape[1]
    xp = jnp.pad(x, ((0, 0), (CONV_WIDTH - 1, 0), (0, 0)))
    y = b
    for k in range(CONV_WIDTH):
        y = y + xp[:, k:k + S] * w[k]
    return y

def rglru_mixer(h, w_in, conv_w, conv_b, w_r, b_r, w_i, b_i, lam, w_out):
    B, S, _ = h.shape
    u = h @ w_in
    gate_branch, x_branch = jnp.split(u, 2, axis=-1)
    gate_branch = jax.nn.gelu(gate_branch)
    xc = causal_depthwise_conv(x_branch, conv_w, conv_b)
    xb = xc.reshape(B, S, LRU_BLOCKS, LRU_BLOCK_DIM)
    r = jax.nn.sigmoid((jnp.einsum('bsnd,nde->bsne', xb, w_r) + b_r).astype(jnp.float32))
    i = jax.nn.sigmoid((jnp.einsum('bsnd,nde->bsne', xb, w_i) + b_i).astype(jnp.float32))
    r = r.reshape(B, S, D_RNN)
    i = i.reshape(B, S, D_RNN)
    log_a = LRU_C * r * jax.nn.log_sigmoid(lam.astype(jnp.float32))
    a = jnp.exp(log_a)
    mult = jnp.sqrt(-jnp.expm1(2.0 * log_a))
    bt = mult * (i * xc.astype(jnp.float32))

    def combine(left, right):
        a_l, b_l = left
        a_r, b_r_ = right
        return a_l * a_r, a_r * b_l + b_r_

    _, hs = lax.associative_scan(combine, (a, bt), axis=1)
    y = gate_branch * hs.astype(h.dtype)
    return y @ w_out

def fox_mixer(h, w_in, b_f, q_gain, k_gain, w_out):
    B, S, _ = h.shape
    u = h @ w_in
    q, k, v, f_logit = jnp.split(u, [D_MODEL, 2 * D_MODEL, 3 * D_MODEL], axis=-1)

    def heads(t):
        return t.reshape(B, S, N_HEADS, HEAD_DIM).transpose(0, 2, 1, 3)

    q = rms_norm(heads(q), q_gain)
    k = rms_norm(heads(k), k_gain)
    v = heads(v)
    log_f = jax.nn.log_sigmoid((f_logit + b_f).astype(jnp.float32))
    c = jnp.cumsum(log_f, axis=1).transpose(0, 2, 1)
    scale = HEAD_DIM ** -0.5
    nb = S // Q_BLOCK
    q_blocks = q.reshape(B, N_HEADS, nb, Q_BLOCK, HEAD_DIM).transpose(2, 0, 1, 3, 4)
    c_blocks = c.reshape(B, N_HEADS, nb, Q_BLOCK).transpose(2, 0, 1, 3)
    k_pos = jnp.arange(S)

    def attend(args):
        qb, cb, blk = args
        q_pos = blk * Q_BLOCK + jnp.arange(Q_BLOCK)
        s = jnp.einsum('bhqd,bhkd->bhqk', qb, k).astype(jnp.float32) * scale
        s = s + cb[..., :, None] - c[:, :, None, :]
        s = jnp.where(k_pos[None, :] <= q_pos[:, None], s, NEG_INF)
        p = jax.nn.softmax(s, axis=-1)
        return jnp.einsum('bhqk,bhkd->bhqd', p.astype(v.dtype), v)

    o = lax.map(attend, (q_blocks, c_blocks, jnp.arange(nb)))
    o = o.transpose(1, 0, 3, 2, 4).reshape(B, S, D_MODEL)
    return o @ w_out

def sq_relu_mlp(h, w1, w2):
    return jnp.square(jax.nn.relu(h @ w1)) @ w2

def first_inputs(seed: int = 0) -> dict:
    key = jax.random.key(seed)
    ks = jax.random.split(key, 20)
    f32 = jnp.float32
    nrm = lambda k, shape, fan_in: jax.random.normal(k, shape, f32) * (fan_in ** -0.5)
    a0 = jax.random.uniform(ks[12], (N_LRU, D_RNN), f32, minval=0.9, maxval=0.999)
    return {
        "x": jax.random.normal(ks[0], (BATCH, SEQ, D_MODEL), f32),
        "mix_norm": 1.0 + 0.02 * jax.random.normal(ks[1], (DEPTH, D_MODEL), f32),
        "mlp_norm": 1.0 + 0.02 * jax.random.normal(ks[2], (DEPTH, D_MODEL), f32),
        "mlp_w1": nrm(ks[3], (DEPTH, D_MODEL, D_FF), D_MODEL),
        "mlp_w2": nrm(ks[4], (DEPTH, D_FF, D_MODEL), D_FF),
        "lru_w_in": nrm(ks[5], (N_LRU, D_MODEL, 2 * D_RNN), D_MODEL),
        "lru_conv_w": nrm(ks[6], (N_LRU, CONV_WIDTH, D_RNN), CONV_WIDTH),
        "lru_conv_b": 0.02 * jax.random.normal(ks[7], (N_LRU, D_RNN), f32),
        "lru_w_r": nrm(ks[8], (N_LRU, LRU_BLOCKS, LRU_BLOCK_DIM, LRU_BLOCK_DIM), LRU_BLOCK_DIM),
        "lru_b_r": 0.1 * jax.random.normal(ks[9], (N_LRU, LRU_BLOCKS, LRU_BLOCK_DIM), f32),
        "lru_w_i": nrm(ks[10], (N_LRU, LRU_BLOCKS, LRU_BLOCK_DIM, LRU_BLOCK_DIM), LRU_BLOCK_DIM),
        "lru_b_i": 0.1 * jax.random.normal(ks[11], (N_LRU, LRU_BLOCKS, LRU_BLOCK_DIM), f32),
        "lru_lambda": jnp.log(a0) - jnp.log1p(-a0),
        "lru_w_out": nrm(ks[13], (N_LRU, D_RNN, D_MODEL), D_RNN),
        "fox_w_in": nrm(ks[14], (N_FOX, D_MODEL, 3 * D_MODEL + N_HEADS), D_MODEL),
        "fox_b_f": jax.random.uniform(ks[15], (N_FOX, N_HEADS), f32, minval=1.0, maxval=6.0),
        "fox_q_gain": 1.0 + 0.02 * jax.random.normal(ks[16], (N_FOX, HEAD_DIM), f32),
        "fox_k_gain": 1.0 + 0.02 * jax.random.normal(ks[17], (N_FOX, HEAD_DIM), f32),
        "fox_w_out": nrm(ks[18], (N_FOX, D_MODEL, D_MODEL), D_MODEL),
    }

def first_block(x, mix_norm, mlp_norm, mlp_w1, mlp_w2, lru_w_in, lru_conv_w, lru_conv_b,
              lru_w_r, lru_b_r, lru_w_i, lru_b_i, lru_lambda, lru_w_out,
              fox_w_in, fox_b_f, fox_q_gain, fox_k_gain, fox_w_out):
    for layer in range(DEPTH):
        h = rms_norm(x, mix_norm[layer])
        j = layer // N_MIXERS
        if layer % N_MIXERS == 0:
            mixed = rglru_mixer(h, lru_w_in[j], lru_conv_w[j], lru_conv_b[j], lru_w_r[j],
                                lru_b_r[j], lru_w_i[j], lru_b_i[j], lru_lambda[j], lru_w_out[j])
        else:
            mixed = fox_mixer(h, fox_w_in[j], fox_b_f[j], fox_q_gain[j], fox_k_gain[j],
                              fox_w_out[j])
        x = x + mixed
        x = x + sq_relu_mlp(rms_norm(x, mlp_norm[layer]), mlp_w1[layer], mlp_w2[layer])
    return x


N_A = DEPTH // 2
N_B = DEPTH - N_A
HEAD_DIM_2 = 64
N_HEADS_2 = D_MODEL // HEAD_DIM_2
N_META = 16
BLOCK = 128
PAD = BLOCK - N_META
D_DECAY_LORA = max(32, int(round(1.8 * D_MODEL ** 0.5 / 32)) * 32)
D_AAA_LORA = max(32, int(round(1.8 * D_MODEL ** 0.5 / 32)) * 32)
D_MV_LORA = max(32, int(round(1.3 * D_MODEL ** 0.5 / 32)) * 32)
D_GATE_LORA = max(32, int(round(0.6 * D_MODEL ** 0.8 / 32)) * 32)
D_FF_2 = int(math.ceil(8 * D_MODEL / 3 / 256)) * 256
CONV_WIDTH_2 = 3
GN_EPS = 64e-5
RMS_EPS = 1e-6


def rms_norm_2(x, g):
    xf = x.astype(jnp.float32)
    y = xf * lax.rsqrt(jnp.mean(xf * xf, axis=-1, keepdims=True) + RMS_EPS) * g.astype(jnp.float32)
    return y.astype(x.dtype)

def token_shift(x):
    return jnp.pad(x, ((0, 0), (1, 0), (0, 0)))[:, :-1]

def conv_glu_ffn(x, w_up, conv_w, conv_b, w_down):
    u = x @ w_up
    c = u.shape[-1]
    u = lax.conv_general_dilated(
        u, conv_w.reshape(CONV_WIDTH_2, 1, c).astype(u.dtype),
        window_strides=(1,), padding=[(CONV_WIDTH_2 - 1, 0)],
        dimension_numbers=('NWC', 'WIO', 'NWC'), feature_group_count=c) + conv_b
    gate, val = jnp.split(u, 2, axis=-1)
    return (jax.nn.silu(gate) * val) @ w_down

def rwkv7_time_mix(x, v_first, v_res, mix, w_r, w_k, w_v, w_o, w0, w1, w2,
                   a0, a1, a2, g1, g2, k_k, k_a, r_k, lnx_g, lnx_b):
    bsz, L, C = x.shape
    f32 = jnp.float32
    xx = token_shift(x) - x
    xr, xw, xk, xv, xa, xg = [x + xx * mix[i] for i in range(6)]
    r = xr @ w_r
    k = xk @ w_k
    v = xv @ w_v
    w_log = -jax.nn.softplus(-(w0 + jnp.tanh(xw @ w1) @ w2)) - 0.5
    a = jax.nn.sigmoid(a0 + (xa @ a1) @ a2)
    g = jax.nn.sigmoid(xg @ g1) @ g2

    def heads(t):
        return t.astype(f32).reshape(bsz, L, N_HEADS_2, HEAD_DIM_2)

    kk = heads(k * k_k)
    kk = kk / jnp.maximum(jnp.linalg.norm(kk, axis=-1, keepdims=True), 1e-12)
    k = k * (1 + (a - 1) * k_a)
    if v_res is None:
        v_first = v
    else:
        v0, v1, v2 = v_res
        v = v + (v_first - v) * jax.nn.sigmoid(v0 + (xv @ v1) @ v2)
    rh, kh, vh, ah = heads(r), heads(k), heads(v), heads(a)
    decay = jnp.exp(-jnp.exp(heads(w_log)))
    seq = tuple(jnp.moveaxis(t, 1, 0) for t in (rh, decay, kh, vh, -kk, kk * ah))

    def step(S, inp):
        r_t, w_t, k_t, v_t, a_t, b_t = inp
        sa = jnp.einsum('bhij,bhj->bhi', S, a_t)
        S = (S * w_t[:, :, None, :] + sa[..., None] * b_t[:, :, None, :]
             + v_t[..., None] * k_t[:, :, None, :])
        return S, jnp.einsum('bhij,bhj->bhi', S, r_t)

    S0 = jnp.zeros((bsz, N_HEADS_2, HEAD_DIM_2, HEAD_DIM_2), f32)
    _, y = lax.scan(step, S0, seq)
    y = jnp.moveaxis(y, 0, 1)
    mu = jnp.mean(y, axis=-1, keepdims=True)
    var = jnp.mean(jnp.square(y - mu), axis=-1, keepdims=True)
    y = ((y - mu) * lax.rsqrt(var + GN_EPS)).reshape(bsz, L, C) * lnx_g.astype(f32) + lnx_b.astype(f32)
    bonus = jnp.sum(rh * kh * r_k.astype(f32), axis=-1, keepdims=True) * vh
    y = (y + bonus.reshape(bsz, L, C)).astype(x.dtype)
    return (y * g) @ w_o, v_first

def to_padded_heads(t):
    bsz, L, _ = t.shape
    t = t.reshape(bsz, L, N_HEADS_2, HEAD_DIM_2)
    t = jnp.pad(t, ((0, 0), (PAD, 0), (0, 0), (0, 0)))
    return jnp.transpose(t, (0, 2, 1, 3))

def stick_breaking_attention(q, k, v):
    bsz, nh, lp, dh = q.shape
    nb = lp // BLOCK
    scale = dh ** -0.5
    key_pos = jnp.arange(lp)
    qb = jnp.moveaxis(q.reshape(bsz, nh, nb, BLOCK, dh), 2, 0)

    def one_block(args):
        q_blk, blk = args
        z = jnp.einsum('bhqd,bhkd->bhqk', q_blk, k).astype(jnp.float32) * scale
        q_pos = blk * BLOCK + jnp.arange(BLOCK)
        valid = (key_pos[None, :] < q_pos[:, None]) & (key_pos[None, :] >= PAD)
        log_1m = jnp.where(valid, jax.nn.log_sigmoid(-z), 0.0)
        log_after = lax.cumsum(log_1m, axis=3, reverse=True) - log_1m
        w = jnp.where(valid, jnp.exp(jax.nn.log_sigmoid(z) + log_after), 0.0)
        return jnp.einsum('bhqk,bhkd->bhqd', w.astype(v.dtype), v)

    out = lax.map(one_block, (qb, jnp.arange(nb)))
    out = jnp.moveaxis(out, 0, 2).reshape(bsz, nh, lp, dh)
    return jnp.transpose(out, (0, 2, 1, 3))[:, PAD:].reshape(bsz, lp - PAD, nh * dh)

def second_inputs(seed: int = 0) -> dict:
    key = jax.random.key(seed)
    ks = jax.random.split(key, 40)
    counter = iter(range(40))

    def nk():
        return ks[next(counter)]

    def nrm(shape, s):
        return jax.random.normal(nk(), shape, jnp.float32) * s

    def uni(shape, lo, hi):
        return jax.random.uniform(nk(), shape, jnp.float32, lo, hi)

    D, F2 = D_MODEL, 2 * D_FF_2
    nv = max(N_A - 1, 0)
    return {
        "x": nrm((BATCH, SEQ, D), 1.0),
        "meta_tokens": nrm((N_META, D), 1.0),
        "norm_mix_g": 1.0 + nrm((DEPTH, D), 0.02),
        "norm_ffn_g": 1.0 + nrm((DEPTH, D), 0.02),
        "ffn_up": nrm((DEPTH, D, F2), D ** -0.5),
        "ffn_conv_w": nrm((DEPTH, CONV_WIDTH_2, F2), CONV_WIDTH_2 ** -0.5),
        "ffn_conv_b": nrm((DEPTH, F2), 0.01),
        "ffn_down": nrm((DEPTH, D_FF_2, D), D_FF_2 ** -0.5),
        "rw_mix": uni((N_A, 6, D), 0.0, 1.0),
        "rw_wr": nrm((N_A, D, D), D ** -0.5),
        "rw_wk": nrm((N_A, D, D), D ** -0.5),
        "rw_wv": nrm((N_A, D, D), D ** -0.5),
        "rw_wo": nrm((N_A, D, D), D ** -0.5),
        "rw_w0": uni((N_A, D), -6.5, -1.0),
        "rw_w1": nrm((N_A, D, D_DECAY_LORA), D ** -0.5),
        "rw_w2": nrm((N_A, D_DECAY_LORA, D), 0.1 * D_DECAY_LORA ** -0.5),
        "rw_a0": nrm((N_A, D), 0.1),
        "rw_a1": nrm((N_A, D, D_AAA_LORA), D ** -0.5),
        "rw_a2": nrm((N_A, D_AAA_LORA, D), 0.1 * D_AAA_LORA ** -0.5),
        "rw_g1": nrm((N_A, D, D_GATE_LORA), D ** -0.5),
        "rw_g2": nrm((N_A, D_GATE_LORA, D), D_GATE_LORA ** -0.5),
        "rw_kk": 0.85 + nrm((N_A, D), 0.05),
        "rw_ka": 1.0 + nrm((N_A, D), 0.05),
        "rw_rk": nrm((N_A, N_HEADS_2, HEAD_DIM_2), 0.1),
        "rw_lnx_g": 1.0 + nrm((N_A, D), 0.02),
        "rw_lnx_b": nrm((N_A, D), 0.01),
        "rw_v0": 1.0 + nrm((nv, D), 0.1),
        "rw_v1": nrm((nv, D, D_MV_LORA), D ** -0.5),
        "rw_v2": nrm((nv, D_MV_LORA, D), 0.1 * D_MV_LORA ** -0.5),
        "kv_norm_g": 1.0 + nrm((D,), 0.02),
        "sb_wk": nrm((D, D), D ** -0.5),
        "sb_wv": nrm((D, D), D ** -0.5),
        "sb_wq": nrm((N_B, D, D), D ** -0.5),
        "sb_wo": nrm((N_B, D, D), D ** -0.5),
        "final_norm_g": 1.0 + nrm((D,), 0.02),
    }

def second_block(x, meta_tokens, norm_mix_g, norm_ffn_g, ffn_up, ffn_conv_w, ffn_conv_b, ffn_down,
              rw_mix, rw_wr, rw_wk, rw_wv, rw_wo, rw_w0, rw_w1, rw_w2, rw_a0, rw_a1, rw_a2,
              rw_g1, rw_g2, rw_kk, rw_ka, rw_rk, rw_lnx_g, rw_lnx_b, rw_v0, rw_v1, rw_v2,
              kv_norm_g, sb_wk, sb_wv, sb_wq, sb_wo, final_norm_g):
    bsz = x.shape[0]
    meta = jnp.broadcast_to(meta_tokens.astype(x.dtype)[None], (bsz, N_META, D_MODEL))
    h = jnp.concatenate([meta, x], axis=1)
    v_first = None
    k_sh = v_sh = None
    for layer in range(DEPTH):
        hn = rms_norm_2(h, norm_mix_g[layer])
        if layer < N_A:
            i = layer
            v_res = None if i == 0 else (rw_v0[i - 1], rw_v1[i - 1], rw_v2[i - 1])
            mix_out, v_first = rwkv7_time_mix(
                hn, v_first, v_res, rw_mix[i], rw_wr[i], rw_wk[i], rw_wv[i], rw_wo[i],
                rw_w0[i], rw_w1[i], rw_w2[i], rw_a0[i], rw_a1[i], rw_a2[i], rw_g1[i], rw_g2[i],
                rw_kk[i], rw_ka[i], rw_rk[i], rw_lnx_g[i], rw_lnx_b[i])
        else:
            j = layer - N_A
            if layer == N_A:
                kvn = rms_norm_2(h, kv_norm_g)
                k_sh = to_padded_heads(kvn @ sb_wk)
                v_sh = to_padded_heads(kvn @ sb_wv)
            q = to_padded_heads(hn @ sb_wq[j])
            mix_out = stick_breaking_attention(q, k_sh, v_sh) @ sb_wo[j]
        h = h + mix_out
        h = h + conv_glu_ffn(rms_norm_2(h, norm_ffn_g[layer]), ffn_up[layer], ffn_conv_w[layer],
                             ffn_conv_b[layer], ffn_down[layer])
    return rms_norm_2(h, final_norm_g)[:, N_META:, :]


def setup_inputs(seed=0):
    out = dict(first_inputs(seed))
    for name, value in second_inputs(seed + 1).items():
        if name != "x":
            out[name + "_2"] = value
    return out


def reference(
    x, mix_norm, mlp_norm, mlp_w1, mlp_w2, lru_w_in, lru_conv_w, lru_conv_b, lru_w_r, lru_b_r,
    lru_w_i, lru_b_i, lru_lambda, lru_w_out, fox_w_in, fox_b_f, fox_q_gain, fox_k_gain,
    fox_w_out, meta_tokens_2, norm_mix_g_2, norm_ffn_g_2, ffn_up_2, ffn_conv_w_2, ffn_conv_b_2,
    ffn_down_2, rw_mix_2, rw_wr_2, rw_wk_2, rw_wv_2, rw_wo_2, rw_w0_2, rw_w1_2, rw_w2_2,
    rw_a0_2, rw_a1_2, rw_a2_2, rw_g1_2, rw_g2_2, rw_kk_2, rw_ka_2, rw_rk_2, rw_lnx_g_2,
    rw_lnx_b_2, rw_v0_2, rw_v1_2, rw_v2_2, kv_norm_g_2, sb_wk_2, sb_wv_2, sb_wq_2, sb_wo_2,
    final_norm_g_2,
):
    x = first_block(
        x, mix_norm, mlp_norm, mlp_w1, mlp_w2, lru_w_in, lru_conv_w, lru_conv_b, lru_w_r,
        lru_b_r, lru_w_i, lru_b_i, lru_lambda, lru_w_out, fox_w_in, fox_b_f, fox_q_gain,
        fox_k_gain, fox_w_out,
    )
    return second_block(
        x, meta_tokens_2, norm_mix_g_2, norm_ffn_g_2, ffn_up_2, ffn_conv_w_2, ffn_conv_b_2,
        ffn_down_2, rw_mix_2, rw_wr_2, rw_wk_2, rw_wv_2, rw_wo_2, rw_w0_2, rw_w1_2, rw_w2_2,
        rw_a0_2, rw_a1_2, rw_a2_2, rw_g1_2, rw_g2_2, rw_kk_2, rw_ka_2, rw_rk_2, rw_lnx_g_2,
        rw_lnx_b_2, rw_v0_2, rw_v1_2, rw_v2_2, kv_norm_g_2, sb_wk_2, sb_wv_2, sb_wq_2, sb_wo_2,
        final_norm_g_2,
    )


_drawn_inputs = setup_inputs


def setup_inputs(seed=0):
    import zlib

    import numpy as np

    out = dict(_drawn_inputs(seed))
    spreads = {}
    factors = {'mix_norm': 3.589,
     'lru_b_r': 4.889,
     'lru_b_i': 3.22,
     'fox_q_gain': 8.0,
     'fox_k_gain': 8.0,
     'norm_mix_g_2': 5.287,
     'norm_ffn_g_2': 5.079,
     'ffn_conv_b_2': 24.083,
     'rw_w1_2': 8.0,
     'rw_w2_2': 8.0,
     'rw_a0_2': 4.724,
     'rw_a1_2': 4.767,
     'rw_a2_2': 4.781,
     'rw_lnx_g_2': 64.0,
     'rw_lnx_b_2': 64.0,
     'kv_norm_g_2': 29.882,
     'final_norm_g_2': 8.089,
     'rw_kk_2': 2.825}
    for name, (base, spread) in spreads.items():
        noise = np.random.default_rng([zlib.crc32(name.encode()), seed]).standard_normal(out[name].shape)
        drawn = base * np.exp(spread * noise) if base else spread * noise
        out[name] = __import__('jax').numpy.asarray(drawn.astype(out[name].dtype))
    for name, factor in factors.items():
        out[name] = (out[name] * factor).astype(out[name].dtype)
    return out
```

```python
from contextlib import ExitStack

import concourse.bass as bass
from concourse import mybir

F32 = mybir.dt.float32
ALU = mybir.AluOpType
ACT = mybir.ActivationFunctionType
AX = mybir.AxisListType.X

P = 128
D = 1024
KT = D // P
SEQ = 512
META = 16
TOK = SEQ + META
HEADS = 16
HD = 64
EPS = 1e-6
GN_EPS = 64e-5
NEG = -1e30
FF = 4096
FF2 = 2816
UP2 = 2 * FF2
CH = 64
NCH = (TOK + CH - 1) // CH
STOP = None

RING = 4
KC = 11
GW = 256
NB = 4


class Psum:

    def __init__(self):
        self.readers = []
        self.base = {}

    def add(self, name, readers):
        self.base[name] = len(self.readers)
        self.readers += readers

    def read_out(self, g):
        return sum(r == self.readers[g] for r in self.readers[:g + 1])


class Weights:

    def __init__(self):
        self.units = []
        self.base = {}

    def add(self, name, units):
        self.base[name] = len(self.units)
        self.units += units

    def landed(self, u):
        return 16 * sum(len(self.units[v][0]) for v in range(u % RING, u + 1, RING))


class K:
    pass


def tiles(n):
    return (n + P - 1) // P


def plan_product(k, name, src, cols, readers, kc=None):
    rows = src.shape[0]
    nk = tiles(rows)
    kc = kc or min(nk, KC)
    groups = []
    for c0, c1 in cols:
        for c in range(c0, c1, GW):
            groups.append((c, min(GW, c1 - c)))
    nt = sum(tiles(w) for _, w in groups)
    if isinstance(readers, str):
        readers = [readers] * nt
    k.psum.add(name, readers)
    units, done = [], k.psum.base[name]
    for c, w in groups:
        for k0 in range(0, nk, kc):
            nkk = min(kc, nk - k0)
            copies = []
            full = min(rows - k0 * P, nkk * P) // P
            if full:
                copies.append((0, P, 0, full, w, src[k0 * P:(k0 + full) * P, c:c + w].rearrange("(t p) n -> p t n", p=P)))
            if full < nkk:
                left = rows - (k0 + full) * P
                copies.append((0, left, full, full + 1, w, src[(k0 + full) * P:rows, c:c + w].rearrange("(t p) n -> p t n", t=1)))
            last = k0 + nkk == nk
            if last:
                done += tiles(w)
                free = ("full", done)
            else:
                k.n_used += 1
                free = ("used", k.n_used)
            units.append((copies, free))
    k.weights.add(name, units)
    k.products[name] = (rows, nk, kc, groups)


def product(pe, k, name, rhs, ready, after=None, width=None):
    rows, nk, kc, groups = k.products[name]
    g = k.psum.base[name]
    u = k.weights.base[name]
    first = True
    for c, w in groups:
        nt = tiles(w)
        for k0 in range(0, nk, kc):
            nkk = min(kc, nk - k0)
            pe.wait_ge(k.w_landed[u % RING], k.weights.landed(u))
            slot = k.ring[:, u % RING]
            for j in range(nt):
                m = min(P, w - j * P)
                if k0 == 0:
                    take(pe, k, g + j)
                bank = k.pp[(g + j) % NB]
                for kk in range(nkk):
                    kt = k0 + kk
                    kp = min(P, rows - kt * P)
                    if first and j == 0:
                        ready(kt)
                    for h in range(2):
                        r = rhs(kt, h)
                        mm = pe.matmul(bank[0:m, h, 0:r.shape[1]], slot[0:kp, kk, j * P:j * P + m], r,
                                       start=kt == 0, stop=kt == nk - 1)
                if k0 + nkk == nk:
                    mm.then_inc(k.full, 1)
                elif j == nt - 1:
                    mm.then_inc(k.used, 1)
            u += 1
        g += nt
        first = False
        if after:
            after(g)


def take(pe, k, g):
    if g >= NB:
        o = g - NB
        pe.wait_ge(k.read[k.psum.readers[o]], k.psum.read_out(o))


def filled(eng, k, g):
    eng.wait_ge(k.full, g + 1)


def was_read(eng, k, g):
    eng.wait_ge(k.read[k.psum.readers[g]], k.psum.read_out(g))


def freed(k, g, ins):
    ins.then_inc(k.read[k.psum.readers[g]], 1)


def halves(ap):
    return ap.rearrange("p (h n) -> p h n", h=2)


def build(nc, A, out):
    k = K()
    k.nc = nc
    k.A = A
    k.out = out
    k.psum, k.weights, k.products, k.n_used = Psum(), Weights(), {}, 0
    with ExitStack() as ctx:
        def sb(name, shape):
            return ctx.enter_context(nc.sbuf_tensor(name, shape, F32))

        def sem(name):
            return ctx.enter_context(nc.semaphore(name))

        k.sem = sem
        k.pp = [ctx.enter_context(nc.psum_tensor(f"pp{i}", [P, 2, 512], F32)) for i in range(NB)]
        k.bank = [k.pp[i // 2][:, i % 2, :] for i in range(8)]

        k.x = sb("x", [P, KT, TOK])
        k.ident = sb("ident", [P, P])
        k.ones = sb("ones", [P, P])
        k.pair = sb("pair", [P, P])
        k.mask_le = sb("mask_le", [P, P])
        k.mask_lt = sb("mask_lt", [P, P])
        k.par = sb("par", [P, 5 * P])
        k.small = sb("small", [P, 64])
        k.sq = sb("sq", [P, 3, TOK])
        k.rs = sb("rs", [P, TOK])
        k.cm = sb("chunk_masks", [P, 11, CH])
        k.restart = sb("restart", [P, TOK])
        k.parch = sb("chunk_decay", [P, KT, NCH - 1])
        k.NA = (nc.sbuf_bytes_remaining // 4) // 8 * 8
        k.arena = sb("arena", [P, k.NA])
        k.ring = k.arena[:, 0:RING * KC * GW].rearrange("p (s t n) -> p s t n", s=RING, t=KC)
        k.h0 = RING * KC * GW
        k.h = k.arena[:, k.h0:k.h0 + KT * (TOK + 1)].rearrange("p (t n) -> p t n", t=KT)
        k.w0 = k.h0 + KT * (TOK + 1)
        k.NW = k.NA - k.w0

        def work(at, *shape):
            n = 1
            for s in shape:
                n *= s
            assert at + n <= k.NW, (at, n, k.NW)
            v = k.arena[:, k.w0 + at:k.w0 + at + n]
            if len(shape) == 2:
                v = v.rearrange("p (a b) -> p a b", a=shape[0])
            if len(shape) == 3:
                v = v.rearrange("p (a b c) -> p a b c", a=shape[0], b=shape[1])
            return v

        k.work = work

        k.w_landed = [sem(f"w_landed{i}") for i in range(RING)]
        k.used = sem("w_used")
        k.full = sem("psum_full")
        k.read = {"act": sem("read_by_act"), "dve": sem("read_by_dve")}
        k.loaded = sem("loaded")
        k.made = sem("constants_made")
        k.masks = sem("chunk_masks_made")
        k.sq_ready = sem("sq_ready")
        k.sq_used = sem("sq_used")
        k.h_ready = sem("h_ready")
        k.step = sem("dve_step")
        k.stored = sem("stored")

        stages = plan(k)
        block = ctx.enter_context(nc.Block())

        @block.sync
        def _(sp):
            load_inputs(sp, k)
            load_weights(sp, k)
            for s in stages:
                if s.sync:
                    s.sync(sp)

        @block.gpsimd
        def _(pool):
            make_constants(pool, k)
            make_chunk_masks(pool, k)
            for s in stages:
                if s.pool:
                    s.pool(pool)

        @block.tensor
        def _(pe):
            for s in stages:
                if s.pe:
                    s.pe(pe)

        @block.scalar
        def _(act):
            for s in stages:
                if s.act:
                    s.act(act)

        @block.vector
        def _(dve):
            k.n_step = 0
            for s in stages:
                if s.dve:
                    s.dve(dve)


def link(dve, k, ins):
    k.n_step += 1
    ins.then_inc(k.step, 1)
    dve.wait_ge(k.step, k.n_step)


def param_rows(A):
    rows = []

    def vec(name, ap):
        rows.append((name, ap))

    for i in range(2):
        vec(f"mix_norm{i}", A["mix_norm"][i])
        vec(f"mlp_norm{i}", A["mlp_norm"][i])
    for i in range(4):
        vec(f"conv_w{i}", A["lru_conv_w"][0, i])
    vec("conv_b", A["lru_conv_b"][0])
    vec("b_r", A["lru_b_r"][0].rearrange("n e -> (n e)"))
    vec("b_i", A["lru_b_i"][0].rearrange("n e -> (n e)"))
    vec("lam", A["lru_lambda"][0])
    for i in range(2):
        vec(f"norm_mix{i}", A["norm_mix_g_2"][i])
        vec(f"norm_ffn{i}", A["norm_ffn_g_2"][i])
    for i in range(6):
        vec(f"rw_mix{i}", A["rw_mix_2"][0, i])
    for n in ("w0", "a0", "kk", "ka", "lnx_g", "lnx_b"):
        vec("rw_" + n, A[f"rw_{n}_2"][0])
    vec("rw_rk", A["rw_rk_2"][0].rearrange("n e -> (n e)"))
    vec("kv_norm", A["kv_norm_g_2"])
    vec("final_norm", A["final_norm_g_2"])
    for i in range(2):
        for j in range(3):
            vec(f"ffn_w{i}{j}", A["ffn_conv_w_2"][i, j])
        vec(f"ffn_b{i}", A["ffn_conv_b_2"][i])
    return rows


def plan_params(k):
    at, k.col, copies = 0, {}, []
    for name, ap in param_rows(k.A):
        n = ap.shape[0] // P
        k.col[name] = at
        done = 0
        while done < n:
            m = min(n - done, P - at % P)
            copies.append((at // P, at % P, m, ap[done * P:(done + m) * P].rearrange("(r c) -> r c", c=P)))
            at += m
            done += m
    for name in ("fox_q_gain", "fox_k_gain"):
        k.col[name] = at
        for h in range(2):
            copies.append((at // P, at % P, 1, k.A[name], h))
        at += 1
    assert at <= 5 * P
    k.n_rows = at
    k.param_copies = copies


def pcol(k, name, t=0):
    return k.par[:, k.col[name] + t:k.col[name] + t + 1]


class Stage:
    def __init__(self, pe=None, act=None, dve=None, pool=None, sync=None):
        self.pe, self.act, self.dve, self.pool, self.sync = pe, act, dve, pool, sync


def load_inputs(sp, k):
    sp.wait_ge(k.made, 1)
    for c in k.param_copies:
        if len(c) == 4:
            t, r, m, src = c
            sp.dma_start(k.prow[r:r + m, t, :], src).then_inc(k.loaded, 16)
        else:
            t, r, m, src, h = c
            sp.dma_start(k.prow[r:r + 1, t, h * HD:(h + 1) * HD], src).then_inc(k.loaded, 16)
    for t in range(4):
        sp.dma_start(k.xrow[:, t, :], k.A["x"][0, t * P:(t + 1) * P, :]).then_inc(k.loaded, 16)
    sp.dma_start(k.mrow[0:META, :], k.A["meta_tokens_2"]).then_inc(k.loaded, 16)
    sp.dma_start(k.small[0:HEADS, 48:49], k.A["fox_b_f"].rearrange("a n -> n a")).then_inc(k.loaded, 16)
    sp.wait_ge(k.made, 2)
    for j, name in enumerate(("lru_w_r", "lru_w_i")):
        for h in range(2):
            sp.dma_start(k.wri[h * HD:(h + 1) * HD, j, :, h * HD:(h + 1) * HD],
                         k.A[name][0].rearrange("(f h) d e -> h d f e", h=2)[h]).then_inc(k.wri_loaded, 16)
    k.n_loaded = 16 * (len(k.param_copies) + 6)


def load_weights(sp, k):
    for u, (copies, _) in enumerate(k.weights.units):
        if u in k.hold:
            sp.wait_ge(k.hold[u][0], k.hold[u][1])
        if u >= RING:
            what, value = k.weights.units[u - RING][1]
            sp.wait_ge(k.full if what == "full" else k.used, value)
        for p0, p1, t0, t1, w, src in copies:
            sp.dma_start(k.ring[p0:p1, u % RING, t0:t1, 0:w], src).then_inc(k.w_landed[u % RING], 16)


def make_constants(pool, k):
    pool.memset(k.prow, 0.0).then_inc(k.made, 1)
    pool.memset(k.wri, 0.0).then_inc(k.made, 1)
    pool.memset(k.ones[:, :], 1.0).then_inc(k.made, 1)
    pool.memset(k.ident[:, :], 0.0).then_inc(k.made, 1)
    pool.memset(k.pair[:, :], 0.0).then_inc(k.made, 1)
    pool.memset(k.mask_le[:, :], 0.0).then_inc(k.made, 1)
    pool.memset(k.mask_lt[:, :], 0.0).then_inc(k.made, 1)
    pool.memset(k.small[:, 40:41], EPS).then_inc(k.made, 1)
    pool.memset(k.small[:, 41:42], GN_EPS).then_inc(k.made, 1)
    pool.memset(k.h[:, :, 0:1], 0.0).then_inc(k.made, 1)
    pool.wait_ge(k.made, 10)
    pool.affine_select(out=k.ident[:, :], in_=k.ident[:, :], compare_op=ALU.not_equal, fill=1.0, base=0,
                       pattern=[[-1, P]], channel_multiplier=1).then_inc(k.made, 1)
    pool.affine_select(out=k.mask_le[:, :], in_=k.mask_le[:, :], compare_op=ALU.is_ge, fill=NEG, base=0,
                       pattern=[[-1, P]], channel_multiplier=1).then_inc(k.made, 1)
    pool.affine_select(out=k.mask_lt[:, :], in_=k.mask_lt[:, :], compare_op=ALU.is_gt, fill=NEG, base=0,
                       pattern=[[-1, P]], channel_multiplier=1).then_inc(k.made, 1)
    for h in range(2):
        pool.wait_ge(k.made, 13 + h)
        pool.memset(k.pair[h * HD:(h + 1) * HD, h * HD:(h + 1) * HD], 1.0).then_inc(k.made, 1)
    pool.wait_ge(k.made, MADE)


MADE = 15


LOWER, UPPER, UPPER_EQ, ONE_LOW, ONE_UP, EYE = 0, 1, 2, 3, 4, 10
LEVELS = [2, 4, 8, 16, 32]


def make_chunk_masks(pool, k):
    m = k.cm
    pool.memset(m[:, 0:3, :], 1.0).then_inc(k.masks, 1)
    pool.memset(m[:, 3:11, :], 0.0).then_inc(k.masks, 1)
    pool.memset(k.restart[:, :], 1.0).then_inc(k.masks, 1)
    pool.wait_ge(k.masks, 3)
    n = 3
    pool.memset(k.restart[:, 0:TOK:CH], 0.0).then_inc(k.masks, 1)
    pool.memset(m[:, ONE_LOW, 0:CH:2], 1.0).then_inc(k.masks, 1)
    pool.memset(m[:, ONE_UP, 1:CH:2], 1.0).then_inc(k.masks, 1)
    n += 3
    for l, b in enumerate(LEVELS):
        pool.memset(m[:, 5 + l, :].rearrange("p (n h i) -> p n h i", h=2, i=b)[:, :, 1, :], 1.0).then_inc(k.masks, 1)
        n += 1
    for h in range(2):
        def keep(at, op, base, pattern, row, fill=0.0):
            nonlocal n
            pool.wait_ge(k.masks, n)
            v = m[h * HD:(h + 1) * HD, at, :]
            pool.affine_select(out=v, in_=v, compare_op=op, fill=fill, base=base, pattern=pattern,
                               channel_multiplier=row).then_inc(k.masks, 1)
            n += 1
        keep(LOWER, ALU.is_gt, 0, [[-1, CH]], 1)
        keep(UPPER, ALU.is_gt, 0, [[1, CH]], -1)
        keep(UPPER_EQ, ALU.is_ge, 0, [[1, CH]], -1)
        keep(ONE_LOW, ALU.is_equal, -1, [[-1, CH]], 1)
        keep(ONE_UP, ALU.is_equal, -1, [[1, CH]], -1)
        keep(EYE, ALU.not_equal, 0, [[-1, CH]], 1, 1.0)
        for l, b in enumerate(LEVELS):
            nb = CH // (2 * b)
            keep(5 + l, ALU.is_ge, 0, [[-2 * b, nb], [0, 2 * b]], 1)
            keep(5 + l, ALU.is_ge, b - 1, [[2 * b, nb], [0, 2 * b]], -1)
    k.n_masks = n
    pool.wait_ge(k.masks, n)


N_MASKS = 3 + 3 + len(LEVELS) + 2 * (6 + 2 * len(LEVELS))


def stage_turn_inputs(k):
    k.psum.add("params", ["dve"])
    k.psum.add("x_in", ["dve", "act"] * (KT // 2))
    k.psum.add("meta_in", ["dve"])
    gp, gx, gm = (k.psum.base[n] for n in ("params", "x_in", "meta_in"))

    def pe(e):
        e.wait_ge(k.loaded, 16 * (len(k.param_copies) + 6))
        e.wait_ge(k.made, MADE)
        for t in range(5):
            mm = e.transpose(k.pp[gp % NB][:, t // 4, (t % 4) * P:(t % 4 + 1) * P], k.prow[:, t, :], k.ident[:, :])
        mm.then_inc(k.full, 1)
        for f in range(KT):
            take(e, k, gx + f)
            for t in range(4):
                mm = e.transpose(k.pp[(gx + f) % NB][:, t // 2, (t % 2) * P:(t % 2 + 1) * P],
                                 k.xrow[:, t, f * P:(f + 1) * P], k.ident[:, :])
            mm.then_inc(k.full, 1)
        take(e, k, gm)
        for f in range(KT):
            mm = e.transpose(k.pp[gm % NB][:, 0, f * META:(f + 1) * META], k.mrow[0:META, f * P:(f + 1) * P],
                             k.ident[0:META, 0:META])
        mm.then_inc(k.full, 1)

    def dve(e):
        filled(e, k, gp)
        link(e, k, e.tensor_copy(k.par[:, 0:512], k.pp[gp % NB][:, 0, :]))
        freed(k, gp, e.tensor_copy(k.par[:, 512:640], k.pp[gp % NB][:, 1, 0:P]))
        for f in range(0, KT, 2):
            filled(e, k, gx + f)
            freed(k, gx + f, e.tensor_copy(halves(k.x[:, f, META:TOK]), k.pp[(gx + f) % NB][:, :, 0:256]))
        filled(e, k, gm)
        freed(k, gm, e.tensor_copy(k.x[:, :, 0:META], k.pp[gm % NB][:, 0, 0:P].rearrange("p (f n) -> p f n", f=KT)))

    def act(e):
        e.wait_ge(k.made, MADE)
        for f in range(1, KT, 2):
            filled(e, k, gx + f)
            freed(k, gx + f, e.copy(halves(k.x[:, f, META:TOK]), k.pp[(gx + f) % NB][:, :, 0:256]))

    k.x_ready = [gx + f for f in range(KT)]
    return Stage(pe, act, dve)


def stage_norm(k, gains, t0, outs=None):
    n = k.n_norm
    k.n_norm += 1
    name = f"norm{n}"
    k.psum.add(name, ["act"])
    g = k.psum.base[name]
    W = TOK - t0
    src = k.x_before = list(k.x_ready)
    k.h_base = base = k.n_h
    k.n_h += KT * len(gains)
    outs = outs or [k.h[:, :, 1:TOK + 1]]
    hw = W // 2

    def act(e):
        for f in range(KT):
            was_read(e, k, src[f])
            if f >= 3:
                e.wait_ge(k.sq_used, (KT - 1) * n + f - 2)
            e.activation(k.sq[:, f % 3, 0:W], k.x[:, f, t0:TOK], ACT.Square).then_inc(k.sq_ready, 1)
        filled(e, k, g)
        freed(k, g, e.activation(halves(k.rs[:, 0:W]), k.pp[g % NB][:, :, 0:hw], ACT.Sqrt, bias=k.small[:, 40:41], scale=1.0 / D))

    def pe(e):
        take(e, k, g)
        for f in range(KT):
            e.wait_ge(k.sq_ready, KT * n + f + 1)
            for h in range(2):
                mm = e.matmul(k.pp[g % NB][:, h, 0:hw], k.ones[:, :], k.sq[:, f % 3, h * hw:(h + 1) * hw],
                              start=f == 0, stop=f == KT - 1)
            mm.then_inc(k.sq_used if f < KT - 1 else k.full, 1)

    def dve(e):
        was_read(e, k, g)
        link(e, k, e.reciprocal(k.rs[:, 0:W], k.rs[:, 0:W]))
        for gain, o in zip(gains, outs):
            for f in range(KT):
                e.scalar_tensor_tensor(o[:, f, t0:TOK], k.x[:, f, t0:TOK], pcol(k, gain, f), k.rs[:, 0:W],
                                       ALU.mult, ALU.mult).then_inc(k.h_ready, 1)

    return Stage(pe, act, dve)


def h_tile(k, t0, src=None):
    src = src if src is not None else k.h[:, :, 1:TOK + 1]
    hw = (TOK - t0) // 2
    return lambda kt, h: src[:, kt, t0 + h * hw:t0 + (h + 1) * hw]


def h_wait(pe, k, base):
    return lambda kt: pe.wait_ge(k.h_ready, base + kt + 1)


def residual(k, name, t0):
    g = k.psum.base[name]
    hw = (TOK - t0) // 2
    k.x_ready = [g + f for f in range(KT)]

    def dve(e):
        for f in range(KT):
            filled(e, k, g + f)
            xf = halves(k.x[:, f, t0:TOK])
            freed(k, g + f, e.tensor_tensor(xf, k.pp[(g + f) % NB][:, :, 0:hw], xf, ALU.add))
    return dve


def stage_lru(k):
    t0, hw = META, SEQ // 2
    w_in, w_out = k.A["lru_w_in"][0], k.A["lru_w_out"][0]
    hb = k.h_base
    plan_product(k, "lru_x", w_in, [(D, 2 * D)], "act")
    k.psum.add("lru_ri", ["act"] * (2 * KT))
    plan_product(k, "lru_gate", w_in, [(0, D)], "act")
    plan_product(k, "lru_out", w_out, [(0, D)], "dve")
    gx, gr, gg = (k.psum.base[n] for n in ("lru_x", "lru_ri", "lru_gate"))
    xb, xc, r, i, T, gate = k.xb, k.xc, k.lr, k.li, k.lT, k.lgate
    made, lam_s, conv, ix_s, ta, m2_s, ms_s, gelu, y_s = (k.sem("lru_" + n) for n in (
        "pad", "lam", "conv_ready", "ix_ready", "exp_ready", "m2_ready", "m_ready", "gelu_ready", "y_ready"))
    c8 = k.small[:, 0:8]
    nc8 = k.small[:, 8:16]
    la = k.small[:, 16:24]
    le = k.small[:, 24:32]
    lam = k.par[:, k.col["lam"]:k.col["lam"] + KT]

    def pe(e):
        product(e, k, "lru_x", h_tile(k, t0), h_wait(e, k, hb))
        e.wait_ge(k.wri_loaded, 64)
        for f in range(KT):
            e.wait_ge(conv, f + 1)
            for j in range(2):
                g = gr + 2 * f + j
                take(e, k, g)
                for h in range(2):
                    mm = e.matmul(k.pp[g % NB][:, h, 0:hw], k.wri[:, j, f, :], xc[:, f, h * hw:(h + 1) * hw],
                                  start=True, stop=True)
                mm.then_inc(k.full, 1)
        product(e, k, "lru_gate", h_tile(k, t0), lambda kt: None)
        product(e, k, "lru_out", lambda kt, h: gate[:, kt, h * hw:(h + 1) * hw], lambda kt: e.wait_ge(y_s, kt + 1))

    def act(e):
        was_read(e, k, k.psum.base["params"])
        e.activation(la, lam, ACT.Abs).then_inc(lam_s, 1)
        e.wait_ge(lam_s, 1)
        e.activation(le, la, ACT.Exp, scale=-1.0).then_inc(lam_s, 1)
        e.wait_ge(lam_s, 2)
        e.activation(la, le, ACT.Ln, bias=1.0).then_inc(lam_s, 1)
        for f in range(KT):
            filled(e, k, gx + f)
            freed(k, gx + f, e.copy(halves(xb[:, f, 3:3 + SEQ]), k.pp[(gx + f) % NB][:, :, 0:hw]))
        for f in range(KT):
            for j, (o, b) in enumerate(((r, "b_r"), (i, "b_i"))):
                g = gr + 2 * f + j
                filled(e, k, g)
                freed(k, g, e.activation(halves(o[:, f, :]), k.pp[g % NB][:, :, 0:hw], ACT.Sigmoid,
                                         bias=pcol(k, b, f)))
        e.wait_ge(lam_s, 5)
        was_read(e, k, gr + 2 * KT - 1)
        for f in range(KT):
            e.activation(T[:, f, :], r[:, f, :], ACT.Tanh, scale=nc8[:, f:f + 1]).then_inc(ta, 1)
            e.wait_ge(ta, 2 * f + 1)
            e.activation(r[:, f, :], r[:, f, :], ACT.Exp, scale=c8[:, f:f + 1]).then_inc(ta, 1)
        for f in range(KT):
            filled(e, k, gg + f)
            freed(k, gg + f, e.copy(halves(gate[:, f, :]), k.pp[(gg + f) % NB][:, :, 0:hw]))
            e.wait_ge(m2_s, f + 1)
            e.activation(T[:, f, :], T[:, f, :], ACT.Sqrt).then_inc(ms_s, 1)
        was_read(e, k, gg + KT - 1)
        for f in range(KT):
            e.activation(gate[:, f, :], gate[:, f, :], ACT.Gelu_apprx_tanh).then_inc(gelu, 1)

    def dve(e):
        e.wait_ge(lam_s, 3)
        link(e, k, e.tensor_scalar(le, lam, 0.0, None, ALU.min))
        link(e, k, e.tensor_tensor(le, le, la, ALU.subtract))
        e.tensor_scalar(c8, le, 8.0, None, ALU.mult).then_inc(lam_s, 1)
        e.tensor_scalar(nc8, le, -8.0, None, ALU.mult).then_inc(lam_s, 1)
        e.wait_ge(made, 1)
        for f in range(KT):
            was_read(e, k, gx + f)
            link(e, k, e.tensor_scalar(xc[:, f, :], xb[:, f, 0:SEQ], pcol(k, "conv_w0", f), pcol(k, "conv_b", f),
                                       ALU.mult, ALU.add))
            for j in range(1, 4):
                op = e.scalar_tensor_tensor(xc[:, f, :], xb[:, f, j:j + SEQ], pcol(k, f"conv_w{j}", f), xc[:, f, :],
                                            ALU.mult, ALU.add)
                if j < 3:
                    link(e, k, op)
            op.then_inc(conv, 1)

        def scan(f):
            e.wait_ge(ms_s, f + 1)
            e.wait_ge(ix_s, f + 1)
            link(e, k, e.tensor_tensor(i[:, f, :], i[:, f, :], T[:, f, :], ALU.mult))
            link(e, k, e.tensor_tensor_scan(xc[:, f, :], r[:, f, :], i[:, f, :], 0.0, ALU.mult, ALU.add))

        for f in range(KT):
            e.wait_ge(ta, 2 * f + 2)
            if f:
                e.wait_ge(m2_s, f)
            link(e, k, e.tensor_scalar(k.ld[:, :], T[:, f, :], 1.0, None, ALU.add))
            link(e, k, e.reciprocal(k.ld[:, :], k.ld[:, :]))
            e.scalar_tensor_tensor(T[:, f, :], T[:, f, :], 2.0, k.ld[:, :], ALU.mult, ALU.mult).then_inc(m2_s, 1)
            if f >= 2:
                scan(f - 2)
        scan(KT - 2)
        scan(KT - 1)
        for f in range(KT):
            e.wait_ge(gelu, f + 1)
            e.tensor_tensor(gate[:, f, :], gate[:, f, :], xc[:, f, :], ALU.mult).then_inc(y_s, 1)
        residual_lru(e)

    def pool(e):
        e.memset(xb[:, :, 0:3], 0.0).then_inc(made, 1)
        for f in range(KT):
            was_read(e, k, gr + 2 * f + 1)
            e.wait_ge(conv, f + 1)
            e.tensor_tensor(i[:, f, :], i[:, f, :], xc[:, f, :], ALU.mult).then_inc(ix_s, 1)

    residual_lru = residual(k, "lru_out", t0)
    return Stage(pe, act, dve, pool)


def stage_mlp(k, l):
    t0, hw = META, SEQ // 2
    hb = k.h_base
    NF = FF // P
    up, down = f"mlp_up{l}", f"mlp_down{l}"
    plan_product(k, up, k.A["mlp_w1"][l], [(0, FF)], "act")
    plan_product(k, down, k.A["mlp_w2"][l], [(0, D)], "dve", kc=8)
    g = k.psum.base[up]
    hid = k.work(0, NF, SEQ)
    squared = k.sem(f"mlp_squared{l}")

    def pe(e):
        product(e, k, up, h_tile(k, t0), h_wait(e, k, hb))
        product(e, k, down, lambda kt, h: hid[:, kt, h * hw:(h + 1) * hw], lambda kt: e.wait_ge(squared, kt + 1))

    def act(e):
        for f in range(NF):
            filled(e, k, g + f)
            freed(k, g + f, e.activation(halves(hid[:, f, :]), k.pp[(g + f) % NB][:, :, 0:hw], ACT.Relu))

    def pool(e):
        for f in range(NF):
            was_read(e, k, g + f)
            e.tensor_tensor(hid[:, f, :], hid[:, f, :], hid[:, f, :], ALU.mult).then_inc(squared, 1)

    return Stage(pe, act, residual(k, down, t0), pool)


def plan_tokens(k, name, src, cols, spans, readers):
    n = (len(spans) + 1) // 2
    units, groups = [], list(range(cols[0], cols[1], GW))
    k.psum.add(name, [readers[j % len(readers)] for j in range(n * len(groups))])
    done = k.psum.base[name]
    for c in groups:
        done += n
        units.append(([(0, P, 0, KT, GW, src[:, c:c + GW].rearrange("(t p) n -> p t n", p=P))], ("full", done)))
    k.weights.add(name, units)
    k.products[name] = (groups, spans, n)


def product_tokens(pe, k, name, stationary, ready):
    groups, spans, n = k.products[name]
    g, u = k.psum.base[name], k.weights.base[name]
    for c in groups:
        pe.wait_ge(k.w_landed[u % RING], k.weights.landed(u))
        for j, (a, b) in enumerate(spans):
            if j % 2 == 0:
                take(pe, k, g)
            for kt in range(KT):
                ready(kt)
                mm = pe.matmul(k.pp[g % NB][0:b - a, j % 2, 0:GW], stationary(kt, a, b), k.ring[:, u % RING, kt, 0:GW],
                               start=kt == 0, stop=kt == KT - 1)
            if j % 2 or j == len(spans) - 1:
                mm.then_inc(k.full, 1)
                g += 1
        u += 1


def read_tokens(k, name, eng, me, v):
    groups, spans, n = k.products[name]
    g = k.psum.base[name]
    for c in range(len(groups)):
        for j in range(0, len(spans), 2):
            if k.psum.readers[g] == me:
                filled(eng, k, g)
                copy = eng.copy if me == "act" else eng.tensor_copy
                pair = spans[j:j + 2]
                rows = [b - a for a, b in pair]
                if len(pair) == 2 and rows[0] == rows[1]:
                    freed(k, g, copy(v[0:rows[0], j:j + 2, c * GW:(c + 1) * GW], k.pp[g % NB][0:rows[0], :, 0:GW]))
                else:
                    for h, m in enumerate(rows):
                        op = copy(v[0:m, j + h, c * GW:(c + 1) * GW], k.pp[g % NB][0:m, h, 0:GW])
                    freed(k, g, op)
            g += 1


def stage_fox(k):
    t0, hw = META, SEQ // 2
    w_in, w_out = k.A["fox_w_in"][0], k.A["fox_w_out"][0]
    hb = k.h_base
    spans = [(META + t * P, META + (t + 1) * P) for t in range(4)]
    NG = 2 * D // GW
    plan_product(k, "fox_f", w_in, [(3 * D, 3 * D + HEADS)], "act")
    for u in range(NG):
        plan_product(k, f"fox_qk{u}", w_in, [(u * GW, (u + 1) * GW)], "act")
        if u:
            k.psum.add(f"fox_sum{u - 1}", ["act"] * 2)
    plan_tokens(k, "fox_v", w_in, (2 * D, 3 * D), spans, ["act", "dve"])
    k.psum.add(f"fox_sum{NG - 1}", ["act"] * 2)
    last_tile = len(k.psum.readers)
    plan_product(k, "fox_out", w_out, [(0, D)], "dve")

    at = 0
    q = k.work(at, KT, 2, SEQ); at += KT * 2 * SEQ
    kT = k.work(at, KT, SEQ); at += KT * SEQ
    v = k.work(at, 4, D); at += 4 * D
    o = k.work(at, KT, SEQ); at += KT * SEQ
    pr = k.work(at, 3, SEQ)
    raw = k.work(at, 4, SEQ); at += 4 * SEQ
    pT = k.work(at, 3, SEQ)
    sq = k.work(at, 4, SEQ); at += 4 * SEQ
    zf, az = o[:, 0, :], o[:, 1, :]
    c = k.work(at, SEQ); at += SEQ
    nm = k.work(at, 64); at += 64
    tot = k.work(at, 64); at += 64
    rt = k.work(at, 64); at += 64
    rsq = k.sq

    zero, f_s, c_s, raw_s, qk_s = (k.sem("fox_" + n) for n in (
        "q_zeroed", "f_logit", "decay_ready", "raw_ready", "qk_ready"))
    s_full, p_s, t_full, o_full, e_s, pt_s, max_s, o_s = (k.sem("att_" + n) for n in (
        "scores", "p_ready", "turned", "o_full", "exp_done", "pt_ready", "max_ready", "o_read"))
    steps = [(h, i) for h in range(HEADS) for i in range(4)]
    N = len(steps)

    def pe(e):
        product(e, k, "fox_f", h_tile(k, t0), h_wait(e, k, hb))

        def sums(u):
            for j in range(2):
                t, g = 2 * u + j, k.psum.base[f"fox_sum{u}"] + j
                take(e, k, g)
                was_read(e, k, k.psum.base[f"fox_qk{u}"] + j)
                for h in range(2):
                    mm = e.matmul(k.pp[g % NB][:, h, 0:hw], k.pair[:, :], sq[:, t % 4, h * hw:(h + 1) * hw],
                                  start=True, stop=True)
                mm.then_inc(k.full, 1)

        for u in range(NG):
            product(e, k, f"fox_qk{u}", h_tile(k, t0), lambda kt: None)
            if u:
                sums(u - 1)
        product_tokens(e, k, "fox_v", lambda kt, a, b: k.h[:, kt, 1 + a:1 + b], lambda kt: None)
        sums(NG - 1)

        for g in range(last_tile - NB, last_tile):
            was_read(e, k, g)
        e.wait_ge(qk_s, 2 * KT)
        e.wait_ge(c_s, 1)

        def scores(n):
            h, i = steps[n]
            K_ = (i + 1) * P
            if n >= 3:
                e.wait_ge(e_s, n - 2)
            b = k.bank[n % 3][:, 0:K_]
            e.matmul(b, q[:, h // 2, h % 2, i * P:(i + 1) * P], kT[:, h // 2, 0:K_], start=True, stop=False)
            e.matmul(b, k.ident[0:HEADS, h:h + 1].to_broadcast([HEADS, P]), c[0:HEADS, 0:K_], start=False, stop=False)
            e.matmul(b[:, i * P:K_], k.ident[:, :], k.mask_le[:, :], start=False, stop=True).then_inc(s_full, 1)

        def turn(n):
            h, i = steps[n]
            e.wait_ge(p_s, n + 1)
            if n >= 3:
                e.wait_ge(pt_s, n - 2)
            for j in range(i + 1):
                mm = e.transpose(k.bank[3 + n % 3][:, j * P:(j + 1) * P], pr[:, n % 3, j * P:(j + 1) * P], k.ident[:, :])
            mm.then_inc(t_full, 1)

        def values(n):
            h, i = steps[n]
            e.wait_ge(pt_s, n + 1)
            if n >= 2:
                e.wait_ge(o_s, n - 1)
            r = h % 2 * HD
            for j in range(i + 1):
                mm = e.matmul(k.bank[6 + n % 2][r:r + HD, 0:P], v[:, j, h * HD:(h + 1) * HD],
                              pT[:, n % 3, j * P:(j + 1) * P], start=j == 0, stop=j == i)
            mm.then_inc(o_full, 1)

        for n in range(N + 3):
            if n < N:
                scores(n)
            if 0 <= n - 2 < N:
                turn(n - 2)
            if 0 <= n - 3 < N:
                values(n - 3)
        product(e, k, "fox_out", lambda kt, h: o[:, kt, h * hw:(h + 1) * hw], lambda kt: e.wait_ge(o_s, 8 * (kt + 1)))

    def act(e):
        g = k.psum.base["fox_f"]
        filled(e, k, g)
        e.activation(halves(az[0:HEADS, :]), k.pp[g % NB][0:HEADS, :, 0:hw], ACT.Abs, bias=k.small[0:HEADS, 48:49]).then_inc(f_s, 1)
        freed(k, g, e.activation(halves(zf[0:HEADS, :]), k.pp[g % NB][0:HEADS, :, 0:hw], ACT.Identity, bias=k.small[0:HEADS, 48:49]))
        e.wait_ge(f_s, 1)
        e.activation(az[0:HEADS, :], az[0:HEADS, :], ACT.Exp, scale=-1.0).then_inc(f_s, 1)
        e.wait_ge(f_s, 2)
        e.activation(az[0:HEADS, :], az[0:HEADS, :], ACT.Ln, bias=1.0).then_inc(f_s, 1)

        def roots(u):
            for j in range(2):
                t, g = 2 * u + j, k.psum.base[f"fox_sum{u}"] + j
                filled(e, k, g)
                if t >= 3:
                    e.wait_ge(qk_s, t - 2)
                freed(k, g, e.activation(halves(rsq[:, t % 3, 0:SEQ]), k.pp[g % NB][:, :, 0:hw], ACT.Sqrt,
                                         bias=k.small[:, 40:41], scale=1.0 / HD))

        for u in range(NG):
            for j in range(2):
                t, g = 2 * u + j, k.psum.base[f"fox_qk{u}"] + j
                filled(e, k, g)
                if t >= 4:
                    e.wait_ge(qk_s, t - 3)
                e.activation(halves(raw[:, t % 4, :]), k.pp[g % NB][:, :, 0:hw], ACT.Copy).then_inc(raw_s, 1)
                if t >= 4:
                    gs = k.psum.base[f"fox_sum{(t - 4) // 2}"] + t % 2
                    e.wait_ge(k.full, gs + 1)
                e.wait_ge(raw_s, t + 1)
                freed(k, g, e.activation(halves(sq[:, t % 4, :]), k.pp[g % NB][:, :, 0:hw], ACT.Square))
            if u:
                roots(u - 1)
        read_tokens(k, "fox_v", e, "act", v)
        roots(NG - 1)

        def exps(n):
            h, i = steps[n]
            K_ = (i + 1) * P
            e.wait_ge(max_s, n + 1)
            if n >= 3:
                e.wait_ge(t_full, n - 2)
            e.activation(pr[:, n % 3, 0:K_], k.bank[n % 3][:, 0:K_], ACT.Exp, bias=nm[:, n:n + 1],
                         accum_out=tot[:, n:n + 1]).then_inc(e_s, 1)

        def copies(n):
            h, i = steps[n]
            e.wait_ge(t_full, n + 1)
            if n >= 3:
                e.wait_ge(o_full, n - 2)
            e.copy(pT[:, n % 3, 0:(i + 1) * P], k.bank[3 + n % 3][:, 0:(i + 1) * P]).then_inc(pt_s, 1)

        for n in range(N + 2):
            if n < N:
                exps(n)
            if 0 <= n - 2 < N:
                copies(n - 2)

    def dve(e):
        was_read(e, k, k.psum.base["fox_f"])
        e.wait_ge(f_s, 3)
        link(e, k, e.tensor_scalar(zf[0:HEADS, :], zf[0:HEADS, :], -1.0, 0.0, ALU.mult, ALU.max))
        link(e, k, e.tensor_tensor(zf[0:HEADS, :], zf[0:HEADS, :], az[0:HEADS, :], ALU.add))
        link(e, k, e.memset(az[0:HEADS, :], 1.0))
        e.tensor_tensor_scan(c[0:HEADS, :], az[0:HEADS, :], zf[0:HEADS, :], 0.0, ALU.mult, ALU.add).then_inc(c_s, 1)
        e.wait_ge(zero, 1)
        link(e, k, e.tensor_scalar(k.small[:, 42:43], pcol(k, "fox_q_gain"), HD ** -0.5, None, ALU.mult))
        for u in range(NG):
            if u == NG - 1:
                read_tokens(k, "fox_v", e, "dve", v)
            for j in range(2):
                t, g = 2 * u + j, k.psum.base[f"fox_sum{u}"] + j
                was_read(e, k, g)
                link(e, k, e.reciprocal(rsq[:, t % 3, 0:SEQ], rsq[:, t % 3, 0:SEQ]))
                if t < KT:
                    op0 = e.scalar_tensor_tensor(q[0:HD, t, 0, :], raw[0:HD, t % 4, :], k.small[0:HD, 42:43],
                                                 rsq[0:HD, t % 3, 0:SEQ], ALU.mult, ALU.mult)
                    link(e, k, op0)
                    e.scalar_tensor_tensor(q[HD:P, t, 1, :], raw[HD:P, t % 4, :], k.small[HD:P, 42:43],
                                           rsq[HD:P, t % 3, 0:SEQ], ALU.mult, ALU.mult).then_inc(qk_s, 1)
                else:
                    e.scalar_tensor_tensor(kT[:, t - KT, :], raw[:, t % 4, :], pcol(k, "fox_k_gain"),
                                           rsq[:, t % 3, 0:SEQ], ALU.mult, ALU.mult).then_inc(qk_s, 1)

        def maxima(n):
            h, i = steps[n]
            e.wait_ge(s_full, n + 1)
            e.tensor_reduce(nm[:, n:n + 1], k.bank[n % 3][:, 0:(i + 1) * P], AX, ALU.max, negate=True).then_inc(max_s, 1)

        def scale(n):
            h, i = steps[n]
            e.wait_ge(e_s, n + 1)
            link(e, k, e.reciprocal(rt[:, n:n + 1], tot[:, n:n + 1]))
            e.tensor_scalar(pr[:, n % 3, 0:(i + 1) * P], pr[:, n % 3, 0:(i + 1) * P], rt[:, n:n + 1], None,
                            ALU.mult).then_inc(p_s, 1)

        def outs(n):
            h, i = steps[n]
            e.wait_ge(o_full, n + 1)
            r = h % 2 * HD
            e.tensor_copy(o[r:r + HD, h // 2, i * P:(i + 1) * P], k.bank[6 + n % 2][r:r + HD, 0:P]).then_inc(o_s, 1)

        for n in range(N + 3):
            if n < N:
                maxima(n)
            if 0 <= n - 1 < N:
                scale(n - 1)
            if 0 <= n - 3 < N:
                outs(n - 3)
        add(e)

    def pool(e):
        for g in x_before:
            was_read(e, k, g)
        e.memset(q, 0.0).then_inc(zero, 1)

    x_before = list(k.x_before)
    add = residual(k, "fox_out", t0)
    return Stage(pe, act, dve, pool)


DECAY = 0.6065306597126334


def stage_rwkv_project(k):
    hw = TOK // 2
    hb = k.h_base
    A = k.A
    NG = D // GW
    plan_product(k, "rw_r", A["rw_wr_2"][0], [(0, D)], "act")
    plan_product(k, "rw_k", A["rw_wk_2"][0], [(0, D)], "act")
    for u in range(NG):
        plan_product(k, f"rw_v{u}", A["rw_wv_2"][0], [(u * GW, (u + 1) * GW)], "act")
        k.psum.add(f"rw_ksum{u}", ["act"] * 2)
    plan_product(k, "rw_g1", A["rw_g1_2"][0], [(0, 160)], "act")
    plan_product(k, "rw_w1", A["rw_w1_2"][0], [(0, 64)], "act")
    plan_product(k, "rw_a1", A["rw_a1_2"][0], [(0, 64)], "act")
    plan_product(k, "rw_w2", A["rw_w2_2"][0], [(0, D)], "act")
    plan_product(k, "rw_a2", A["rw_a2_2"][0], [(0, D)], "act")
    k.psum.add("rw_bonus", ["dve"] * KT)
    B = k.psum.base

    r = k.rw_r = k.work(0, KT, TOK)
    kk_ = k.rw_k = k.work(KT * TOK, KT, TOK)
    v = k.rw_v = k.work(2 * KT * TOK, KT, TOK)
    xx = s = k.rw_s = k.work(3 * KT * TOK, KT, TOK)
    xm = k.work(4 * KT * TOK, 12, TOK)
    a = k.rw_a = k.work(4 * KT * TOK, KT, TOK)
    tmp = k.work(5 * KT * TOK, 4, TOK)
    kn = k.rw_y = k.work(5 * KT * TOK + 4 * TOK, KT, TOK)
    mg = k.rw_mg = k.work(6 * KT * TOK + 4 * TOK, 2, TOK)
    mw, ma = k.sq[:, 0, :], k.sq[:, 1, :]
    ht = k.h[:, :, 0:TOK]
    k.pc = k.parch

    xx_s, mix_s, kk_s, sqk_s, kn_s, cum_s, prev_s, ex_s, kp_s, rk_s, fin_s, bb_s, kraw = (k.sem("rw_" + n) for n in (
        "shift_ready", "mix_ready", "kk_ready", "kk_square", "kk_normed", "cum_ready", "prev_ready", "exp_ready",
        "k_ready", "rk_ready", "inputs_ready", "b_ready", "k_raw"))
    k.rw_inputs, k.rw_b = fin_s, bb_s
    MIX = {"r": 0, "k": 1, "v": 2, "g": 3, "w": 4, "a": 5}
    REF = [0, 2, 3, 5, 1, 4]

    def moving(i):
        return lambda kt, h: xm[:, (8 * i + kt) % 12, h * hw:(h + 1) * hw]

    def pe(e):
        def ready(i):
            return lambda kt: e.wait_ge(mix_s, 8 * i + kt + 1)

        def sums(u):
            for j in range(2):
                f, g = 2 * u + j, B[f"rw_ksum{u}"] + j
                take(e, k, g)
                e.wait_ge(sqk_s, f + 1)
                for h in range(2):
                    mm = e.matmul(k.pp[g % NB][:, h, 0:hw], k.pair[:, :], k.sq[:, f % 3, h * hw:(h + 1) * hw],
                                  start=True, stop=True)
                mm.then_inc(k.full, 1)

        product(e, k, "rw_r", moving(0), ready(0))
        product(e, k, "rw_k", moving(1), ready(1))
        for u in range(NG):
            product(e, k, f"rw_v{u}", moving(2), ready(2) if u == 0 else lambda kt: None)
            sums(u)
        product(e, k, "rw_g1", moving(3), ready(3))
        product(e, k, "rw_w1", moving(4), ready(4))
        product(e, k, "rw_a1", moving(5), ready(5))
        product(e, k, "rw_w2", lambda kt, h: mw[0:64, h * hw:(h + 1) * hw], lambda kt: was_read(e, k, B["rw_w1"]))
        product(e, k, "rw_a2", lambda kt, h: ma[0:64, h * hw:(h + 1) * hw], lambda kt: was_read(e, k, B["rw_a1"]))
        for f in range(KT):
            g = B["rw_bonus"] + f
            take(e, k, g)
            e.wait_ge(rk_s, f + 1)
            for h in range(2):
                mm = e.matmul(k.pp[g % NB][:, h, 0:hw], k.pair[:, :], tmp[:, 2 + f % 2, h * hw:(h + 1) * hw],
                              start=True, stop=True)
            mm.then_inc(k.full, 1)

    def act(e):
        for f in range(KT):
            g = B["rw_r"] + f
            filled(e, k, g)
            freed(k, g, e.copy(halves(r[:, f, :]), k.pp[g % NB][:, :, 0:hw]))
        for f in range(KT):
            g = B["rw_k"] + f
            filled(e, k, g)
            freed(k, g, e.copy(halves(kk_[:, f, :]), k.pp[g % NB][:, :, 0:hw]))

        def square(f):
            e.wait_ge(kk_s, f + 1)
            if f >= 3:
                e.wait_ge(k.full, B[f"rw_ksum{(f - 3) // 2}"] + (f - 3) % 2 + 1)
            e.activation(k.sq[:, f % 3, :], kn[:, f, :], ACT.Square).then_inc(sqk_s, 1)

        for u in range(NG):
            for j in range(2):
                square(2 * u + j)
            for j in range(2):
                f, g = 2 * u + j, B[f"rw_v{u}"] + j
                filled(e, k, g)
                freed(k, g, e.copy(halves(v[:, f, :]), k.pp[g % NB][:, :, 0:hw]))
            for j in range(2):
                f, g = 2 * u + j, B[f"rw_ksum{u}"] + j
                filled(e, k, g)
                if f:
                    e.wait_ge(kn_s, f)
                freed(k, g, e.activation(halves(k.rs[:, :]), k.pp[g % NB][:, :, 0:hw], ACT.Sqrt))
        for j, m in enumerate((P, 32)):
            g = B["rw_g1"] + j
            filled(e, k, g)
            freed(k, g, e.activation(halves(mg[0:m, j, :]), k.pp[g % NB][0:m, :, 0:hw], ACT.Sigmoid))
        filled(e, k, B["rw_w1"])
        freed(k, B["rw_w1"], e.activation(halves(mw[0:64, :]), k.pp[B["rw_w1"] % NB][0:64, :, 0:hw], ACT.Tanh))
        filled(e, k, B["rw_a1"])
        freed(k, B["rw_a1"], e.copy(halves(ma[0:64, :]), k.pp[B["rw_a1"] % NB][0:64, :, 0:hw]))
        for name, o, b in (("rw_w2", s, "rw_w0"), ("rw_a2", a, "rw_a0")):
            for f in range(KT):
                g = B[name] + f
                filled(e, k, g)
                freed(k, g, e.activation(halves(o[:, f, :]), k.pp[g % NB][:, :, 0:hw], ACT.Sigmoid, bias=pcol(k, b, f)))
        for f in range(KT):
            e.wait_ge(cum_s, f + 1)
            e.wait_ge(prev_s, f + 1)
            if f >= 2:
                e.wait_ge(fin_s, f - 1)
                e.wait_ge(bb_s, f - 1)
            j = f % 2
            e.activation(ht[:, 2 + j, :], ht[:, j, :], ACT.Exp, scale=-DECAY).then_inc(ex_s, 1)
            e.activation(ht[:, 4 + j, :], ht[:, j, :], ACT.Exp, scale=DECAY).then_inc(ex_s, 1)
            e.activation(ht[:, 6 + j, :], ht[:, 6 + j, :], ACT.Exp, scale=-DECAY).then_inc(ex_s, 1)

    def dve(e):
        for i in range(6):
            for f in range(KT):
                n = 8 * i + f
                if i == 0:
                    e.wait_ge(xx_s, f + 1)
                if n >= 12:
                    last = {0: B["rw_r"] + KT, 1: B["rw_k"] + KT, 2: B[f"rw_v{NG - 1}"] + 2, 3: B["rw_g1"] + 2,
                            4: B["rw_w1"] + 1}[(n - 12) // 8]
                    e.wait_ge(k.full, last)
                e.scalar_tensor_tensor(xm[:, n % 12, :], xx[:, f, :], pcol(k, f"rw_mix{REF[i]}", f), k.h[:, f, 1:TOK + 1],
                                       ALU.mult, ALU.add).then_inc(mix_s, 1)
            if i == 2:
                for f in range(KT):
                    was_read(e, k, B["rw_k"] + f)
                    e.tensor_scalar(kn[:, f, :], kk_[:, f, :], pcol(k, "rw_kk", f), None, ALU.mult).then_inc(kk_s, 1)
                for f in range(KT):
                    g = B[f"rw_ksum{f // 2}"] + f % 2
                    was_read(e, k, g)
                    link(e, k, e.tensor_scalar(k.rs[:, :], k.rs[:, :], 1e-12, None, ALU.max))
                    link(e, k, e.reciprocal(k.rs[:, :], k.rs[:, :]))
                    e.tensor_tensor(kn[:, f, :], kn[:, f, :], k.rs[:, :], ALU.mult).then_inc(kn_s, 1)
        e.wait_ge(k.masks, N_MASKS)
        e.wait_ge(mix_s, 48)
        e.wait_ge(k.full, B["rw_w2"])

        def cum(f):
            was_read(e, k, B["rw_w2"] + f)
            if f >= 2:
                e.wait_ge(ex_s, 3 * (f - 1))
                e.wait_ge(prev_s, f - 1)
            e.tensor_tensor_scan(ht[:, f % 2, :], k.restart[:, :], s[:, f, :], 0.0, ALU.mult, ALU.add).then_inc(cum_s, 1)

        def bonus(f):
            g = B["rw_bonus"] + f
            filled(e, k, g)
            e.wait_ge(bb_s, f + 1)
            e.wait_ge(fin_s, f + 1)
            freed(k, g, e.tensor_tensor(halves(kn[:, f, :]), k.pp[g % NB][:, :, 0:hw], halves(v[:, f, :]), ALU.mult))

        cum(0)
        for f in range(KT):
            j = f % 2
            if f + 1 < KT:
                cum(f + 1)
            was_read(e, k, B["rw_a2"] + f)
            link(e, k, e.tensor_scalar(tmp[:, j, :], a[:, f, :], -1.0, pcol(k, "rw_ka", f), ALU.add, ALU.mult))
            link(e, k, e.scalar_tensor_tensor(kk_[:, f, :], tmp[:, j, :], 1.0, kk_[:, f, :], ALU.add, ALU.mult))
            if f >= 2:
                filled(e, k, B["rw_bonus"] + f - 2)
            e.scalar_tensor_tensor(tmp[:, 2 + j, :], r[:, f, :], pcol(k, "rw_rk", f), kk_[:, f, :], ALU.mult,
                                   ALU.mult).then_inc(rk_s, 1)
            e.wait_ge(rk_s, f + 1)
            e.wait_ge(ex_s, 3 * f + 3)
            link(e, k, e.tensor_tensor(kk_[:, f, :], kk_[:, f, :], ht[:, 4 + j, :], ALU.mult))
            link(e, k, e.tensor_tensor(r[:, f, :], r[:, f, :], ht[:, 2 + j, :], ALU.mult))
            link(e, k, e.tensor_copy(k.pc[:, f, :], ht[:, 2 + j, CH - 1:TOK:CH]))
            e.wait_ge(prev_s, f + 1)
            e.scalar_tensor_tensor(s[:, f, :], kn[:, f, :], -1.0, ht[:, 6 + j, :], ALU.mult, ALU.mult).then_inc(fin_s, 1)
            if f:
                bonus(f - 1)
        bonus(KT - 1)

    def pool(e):
        for f in range(KT):
            e.wait_ge(k.h_ready, hb + f + 1)
            e.tensor_tensor(xx[:, f, :], k.h[:, f, 0:TOK], k.h[:, f, 1:TOK + 1], ALU.subtract).then_inc(xx_s, 1)

        def prev(f):
            e.wait_ge(cum_s, f + 1)
            if f >= 2:
                e.wait_ge(fin_s, f - 1)
            e.tensor_tensor(ht[:, 6 + f % 2, :], ht[:, f % 2, :], s[:, f, :], ALU.subtract).then_inc(prev_s, 1)

        e.wait_ge(kn_s, KT)
        prev(0)
        for f in range(KT):
            j = f % 2
            if f + 1 < KT:
                prev(f + 1)
            was_read(e, k, B["rw_a2"] + f)
            e.wait_ge(rk_s, f + 1)
            e.tensor_tensor(a[:, f, :], a[:, f, :], kn[:, f, :], ALU.mult).then_inc(kraw, 1)
            e.wait_ge(kraw, f + 1)
            e.wait_ge(ex_s, 3 * f + 2)
            e.tensor_tensor(a[:, f, :], a[:, f, :], ht[:, 4 + j, :], ALU.mult).then_inc(bb_s, 1)

    return Stage(pe, act, dve, pool)


PE_ROUNDS = ["LT", "L", "MT", "RB", "RK", "Bt", "Kt", "At", "Vt"]
for _l in range(5):
    PE_ROUNDS += [f"Q{_l}", f"XT{_l}"] + ([f"X{_l}"] if _l < 4 else [])
PE_ROUNDS += ["MV", "WT", "U", "Y", "S"]
DVE_STEPS = ["XT", "L2", "X", "MT2", "RB", "RK"]
for _l in range(5):
    DVE_STEPS += [f"Q{_l}"] + ([f"Q2{_l}"] if _l < 4 else []) + [f"XT{_l}"] + ([f"X{_l}"] if _l < 4 else [])
DVE_STEPS += ["U", "S"]
ACT_STEPS = ["X2", "Bt2", "Kt2", "At2", "Vt2"]
for _l in range(4):
    ACT_STEPS += [f"X2{_l}"]
ACT_STEPS += ["MV", "XT2", "WT2", "U2", "Y", "S2"]
POOL_STEPS = ["B2", "K2", "A2", "V2"]
READER = {"LT": ("dve", "XT"), "L": ("dve", "X"), "MT": ("dve", "MT2"), "RB": ("dve", "RB"), "RK": ("dve", "RK"),
          "Bt": ("act", "Bt2"), "Kt": ("act", "Kt2"), "At": ("act", "At2"), "Vt": ("act", "Vt2"),
          "MV": ("act", "MV"), "WT": ("act", "WT2"), "U": ("dve", "U"), "Y": ("act", "Y"), "S": ("dve", "S")}
for _l in range(5):
    for _n in ("Q", "XT", "X"):
        READER[f"{_n}{_l}"] = ("dve", f"{_n}{_l}")
STEPS = {"pe": PE_ROUNDS, "dve": DVE_STEPS, "act": ACT_STEPS, "pool": POOL_STEPS}
GROUPS = 2


def stage_rwkv_chunks(k):
    G = KT // GROUPS
    sems = {n: k.sem("chunk_" + n) for n in STEPS}
    zero = k.sem("chunk_zeroed")
    big = [k.arena[:, 1024 * i:1024 * (i + 1)] for i in range(15)]
    big += [k.work(5 * KT * TOK + 1024 * i, 1024) for i in range(2)]

    def two(i):
        return big[i].rearrange("p (f n) -> p f n", f=KT)

    def one(i, h):
        return big[i][:, 512 * h:512 * (h + 1)].rearrange("p (f n) -> p f n", f=KT)

    B2, K2, A2, L2, X2, Q2, MT2, Bt2, Kt2, At2, Vt2, S2 = (two(i) for i in range(12))
    V2, XT2, WT2, U2 = Q2, two(12), X2, A2
    S, X, XT, Q, RB, RK, Vt, U = one(13, 0), one(13, 1), one(14, 0), one(14, 1), one(15, 0), one(15, 1), one(16, 0), one(16, 1)
    MV = Q
    tail = k.sq[:, :, :].rearrange("p a b -> p (a b)")[:, 0:1024].rearrange("p (j f n) -> p j f n", j=2, f=KT)
    r, kd, v, a, b, yb = k.rw_r, k.rw_k, k.rw_v, k.rw_s, k.rw_a, k.rw_y
    tail_s = k.sem("chunk_tail")
    last = NCH - 1
    WL = TOK - last * CH

    def value(eng, step, c, g):
        return (c * len(STEPS[eng]) + STEPS[eng].index(step)) * GROUPS + g + 1

    def after(e, eng, step, c, g):
        if c >= 0:
            e.wait_ge(sems[eng], value(eng, step, c, g))

    def done(eng, ins):
        ins.then_inc(sems[eng], 1)

    def width(c):
        return CH if c < last else WL

    def cols(t, c, f):
        return t[:, f, c * CH:c * CH + width(c)]

    def bank_of(c, name, g):
        return k.bank[(value("pe", name, c, g) - 1) % 8]

    def psum(c, name, g, w=CH):
        return bank_of(c, name, g)[:, 0:G * CH].rearrange("p (f n) -> p f n", f=G)[:, :, 0:w]

    def pe(e):
        for g in range(k.rw_tiles - NB, k.rw_tiles):
            was_read(e, k, g)
        e.wait_ge(k.rw_inputs, KT)
        e.wait_ge(zero, k.n_zero)
        order = [(c, n, g) for c in range(NCH) for n in PE_ROUNDS for g in range(GROUPS)]

        def rnd(c, name, terms, w=CH):
            for g in range(GROUPS):
                terms_ready[name](c, g)
                q = value("pe", name, c, g) - 1
                if q >= 8:
                    oc, on, og = order[q - 8]
                    after(e, *READER[on], oc, og)
                for j in range(G):
                    f = g * G + j
                    for i, (st, mv) in enumerate(terms):
                        mm = e.matmul(bank_of(c, name, g)[:, j * CH:j * CH + w], st(f), mv(f), start=i == 0,
                                      stop=i == len(terms) - 1)
                done("pe", mm)

        def t2(t):
            return lambda f: t[:, f, :]

        def at_(c):
            return (lambda f: tail[:, 0, f, :]) if c == last else (lambda f: cols(a, c, f))

        def bt_(c):
            return (lambda f: tail[:, 1, f, :]) if c == last else (lambda f: cols(b, c, f))

        eye = lambda f: k.cm[:, EYE, :]
        W = lambda eng, step: (lambda c, g: after(e, eng, step, c, g))
        both = lambda *ws: (lambda c, g: [x(c, g) for x in ws])
        terms_ready = {
            "LT": both(W("pool", "B2"), lambda c, g: e.wait_ge(tail_s, 1)), "L": W("pool", "A2"), "MT": W("pool", "K2"),
            "RB": W("pool", "B2"), "RK": W("pool", "K2"), "Bt": W("pool", "B2"), "Kt": W("pool", "K2"),
            "At": W("pool", "A2"), "Vt": W("pool", "V2"),
            "MV": both(W("dve", "MT2"), W("act", "Vt2")), "WT": both(W("act", "At2"), W("dve", "XT4")),
            "U": both(W("act", "WT2"), W("act", "XT2"), W("act", "MV"), lambda c, g: after(e, "dve", "S", c - 1, g)),
            "Y": both(W("act", "U2"), W("dve", "RB"), W("dve", "RK"), lambda c, g: after(e, "act", "S2", c - 1, g)),
            "S": both(W("dve", "U"), W("act", "Bt2"), W("act", "Kt2")),
        }
        for l in range(5):
            terms_ready[f"Q{l}"] = both(W("dve", "L2"), W("dve", "XT" if l == 0 else f"XT{l - 1}"))
            terms_ready[f"XT{l}"] = both(W("dve", f"Q{l}"), W("act", "X2" if l == 0 else f"X2{l - 1}"))
            terms_ready[f"X{l}"] = both(W("dve", f"Q2{l}") if l < 4 else W("dve", "Q4"), W("dve", "X" if l == 0 else f"X{l - 1}"))

        for c in range(NCH):
            w = width(c)
            rc = lambda f: cols(r, c, f)
            rnd(c, "LT", [(t2(B2), at_(c))])
            rnd(c, "L", [(t2(A2), bt_(c))])
            rnd(c, "MT", [(t2(K2), at_(c))])
            rnd(c, "RB", [(t2(B2), rc)], w)
            rnd(c, "RK", [(t2(K2), rc)], w)
            rnd(c, "Bt", [(t2(B2), eye)])
            rnd(c, "Kt", [(t2(K2), eye)])
            rnd(c, "At", [(t2(A2), eye)])
            rnd(c, "Vt", [(t2(V2), eye)])
            for l in range(5):
                rnd(c, f"Q{l}", [(t2(L2), t2(XT))])
                rnd(c, f"XT{l}", [(t2(X2), t2(Q))])
                if l < 4:
                    rnd(c, f"X{l}", [(t2(Q2), t2(X))])
            rnd(c, "MV", [(t2(MT2), t2(Vt))])
            rnd(c, "WT", [(t2(At2), t2(XT))])
            rnd(c, "U", [(t2(XT2), t2(MV)), (t2(WT2), t2(S))])
            rnd(c, "Y", [(t2(U2), lambda f: RB[:, f, 0:w]), (t2(Vt2), lambda f: RK[:, f, 0:w]), (t2(S2), rc)], w)
            if c < last:
                rnd(c, "S", [(t2(Bt2), t2(U)), (t2(Kt2), t2(Vt))])

    def group(t, g):
        return t[:, g * G:(g + 1) * G, :]

    def blocks(e, op, dst, src, g, w=CH, after_first=None):
        for h in range(2):
            rows = slice(h * HD, (h + 1) * HD)
            ins = op(dst[rows, g * G:(g + 1) * G, h * CH:h * CH + w], src[rows])
            if h == 0 and after_first:
                after_first(ins)
        return ins

    def dve(e):
        e.wait_ge(zero, k.n_zero)

        def mask(i, n):
            return k.cm[:, i:i + 1, 0:n].to_broadcast([P, G, n])

        def upd(c, name, t, g):
            after(e, "pe", name, c, g)
            done("dve", e.tensor_tensor(group(t, g), psum(c, name, g), group(t, g), ALU.add))

        for c in range(NCH):
            w = width(c)
            for g in range(GROUPS):
                after(e, "pe", "LT", c, g)
                after(e, "pe", "WT", c - 1, g)
                after(e, "act", "XT2", c - 1, g)
                link(e, k, e.tensor_tensor(group(XT, g), psum(c, "LT", g), mask(ONE_UP, CH), ALU.mult))
                done("dve", e.tensor_tensor(group(XT, g), group(XT, g), mask(EYE, CH), ALU.add))
            for g in range(GROUPS):
                after(e, "pe", "L", c, g)
                for h in range(2):
                    rows = slice(h * HD, (h + 1) * HD)
                    ins = e.tensor_tensor(L2[rows, g * G:(g + 1) * G, h * CH:(h + 1) * CH], psum(c, "L", g)[rows],
                                          k.cm[rows, LOWER:LOWER + 1, :].to_broadcast([HD, G, CH]), ALU.mult)
                    if h == 0:
                        link(e, k, ins)
                done("dve", ins)
            for g in range(GROUPS):
                after(e, "pe", "X3", c - 1, g)
                link(e, k, e.tensor_tensor(group(X, g), psum(c, "L", g), mask(ONE_LOW, CH), ALU.mult))
                done("dve", e.tensor_tensor(group(X, g), group(X, g), mask(EYE, CH), ALU.add))
            for g in range(GROUPS):
                after(e, "pe", "MT", c, g)
                after(e, "pe", "MV", c - 1, g)
                for h in range(2):
                    rows = slice(h * HD, (h + 1) * HD)
                    ins = e.tensor_tensor(MT2[rows, g * G:(g + 1) * G, h * CH:(h + 1) * CH], psum(c, "MT", g)[rows],
                                          k.cm[rows, UPPER:UPPER + 1, :].to_broadcast([HD, G, CH]), ALU.mult)
                    if h == 0:
                        link(e, k, ins)
                done("dve", ins)
            for name, t in (("RB", RB), ("RK", RK)):
                for g in range(GROUPS):
                    after(e, "pe", name, c, g)
                    after(e, "pe", "Y", c - 1, g)
                    done("dve", e.tensor_tensor(t[:, g * G:(g + 1) * G, 0:w], psum(c, name, g, w), mask(UPPER_EQ, w), ALU.mult))
            for l in range(5):
                for g in range(GROUPS):
                    after(e, "pe", f"Q{l}", c, g)
                    if l == 0:
                        after(e, "pe", "U", c - 1, g)
                    else:
                        after(e, "pe", f"XT{l - 1}", c, g)
                        after(e, "dve", f"Q2{l - 1}", c, g)
                    done("dve", e.tensor_tensor(group(Q, g), psum(c, f"Q{l}", g), mask(5 + l, CH), ALU.mult))
                if l < 4:
                    for g in range(GROUPS):
                        after(e, "dve", f"Q{l}", c, g)
                        if l == 0:
                            after(e, "pe", "Vt", c, g)
                        else:
                            after(e, "pe", f"X{l - 1}", c, g)
                        for h in range(2):
                            rows = slice(h * HD, (h + 1) * HD)
                            ins = e.tensor_copy(Q2[rows, g * G:(g + 1) * G, h * CH:(h + 1) * CH], group(Q, g)[rows])
                            if h == 0:
                                link(e, k, ins)
                        done("dve", ins)
                for g in range(GROUPS):
                    upd(c, f"XT{l}", XT, g)
                if l < 4:
                    for g in range(GROUPS):
                        if l:
                            after(e, "act", f"X2{l - 1}", c, g)
                        else:
                            after(e, "act", "X2", c, g)
                        upd(c, f"X{l}", X, g)
            for g in range(GROUPS):
                after(e, "pe", "U", c, g)
                after(e, "pe", "S", c - 1, g)
                after(e, "act", "U2", c - 1, g)
                done("dve", e.tensor_copy(group(U, g), psum(c, "U", g)))
            if c < last:
                for g in range(GROUPS):
                    after(e, "pe", "S", c, g)
                    after(e, "act", "S2", c - 1, g)
                    link(e, k, e.tensor_tensor(group(S, g), psum(c, "S", g), group(S, g), ALU.add))
                    done("dve", e.tensor_tensor(group(S, g), group(S, g),
                                                k.pc[:, g * G:(g + 1) * G, c:c + 1].to_broadcast([P, G, CH]), ALU.mult))

    def act(e):
        e.wait_ge(zero, k.n_zero)

        def from_psum(c, name, dst, g, w=CH):
            done("act", blocks(e, e.copy, dst, psum(c, name, g, w), g, w))

        for c in range(NCH):
            w = width(c)

            def x2(l, g):
                after(e, "dve", "X" if l < 0 else f"X{l}", c, g)
                if l >= 0:
                    after(e, "pe", f"XT{l}", c, g)
                else:
                    after(e, "pe", "U", c - 1, g)
                done("act", blocks(e, e.copy, X2, group(X, g), g))

            for g in range(GROUPS):
                x2(-1, g)
            for name, dst, free in (("Bt", Bt2, "S"), ("Kt", Kt2, "S"), ("At", At2, "WT")):
                for g in range(GROUPS):
                    after(e, "pe", name, c, g)
                    after(e, "pe", free, c - 1, g)
                    from_psum(c, name, dst, g)
            for g in range(GROUPS):
                after(e, "pe", "Vt", c, g)
                after(e, "pe", "S", c - 1, g)
                after(e, "pe", "Y", c - 1, g)
                e.copy(group(Vt, g), psum(c, "Vt", g))
                from_psum(c, "Vt", Vt2, g)
            for l in range(4):
                for g in range(GROUPS):
                    x2(l, g)
            for g in range(GROUPS):
                after(e, "pe", "MV", c, g)
                after(e, "pe", "XT4", c, g)
                done("act", e.copy(group(MV, g), psum(c, "MV", g)))
            for g in range(GROUPS):
                after(e, "dve", "XT4", c, g)
                after(e, "pe", "U", c - 1, g)
                done("act", blocks(e, e.copy, XT2, group(XT, g), g))
            for g in range(GROUPS):
                after(e, "pe", "WT", c, g)
                from_psum(c, "WT", WT2, g)
            for g in range(GROUPS):
                after(e, "dve", "U", c, g)
                after(e, "pe", "Y", c - 1, g)
                done("act", blocks(e, e.copy, U2, group(U, g), g))
            for g in range(GROUPS):
                after(e, "pe", "Y", c, g)
                done("act", e.copy(a[:, g * G:(g + 1) * G, c * CH:c * CH + w], psum(c, "Y", g, w)))
            if c < last:
                for g in range(GROUPS):
                    after(e, "dve", "S", c, g)
                    done("act", blocks(e, e.copy, S2, group(S, g), g))

    def pool(e):
        e.wait_ge(k.rw_inputs, KT)
        e.wait_ge(k.rw_b, KT)
        for g in range(k.rw_tiles - NB, k.rw_tiles):
            was_read(e, k, g)
        e.memset(k.arena[:, 0:15 * 1024], 0.0).then_inc(zero, 1)
        e.memset(k.work(5 * KT * TOK, 2048), 0.0).then_inc(zero, 1)
        e.memset(tail, 0.0).then_inc(zero, 1)
        e.wait_ge(zero, 3)
        e.tensor_copy(tail[:, 0, :, 0:WL], a[:, :, last * CH:TOK]).then_inc(zero, 1)
        e.tensor_copy(tail[:, 1, :, 0:WL], b[:, :, last * CH:TOK]).then_inc(tail_s, 1)
        e.wait_ge(zero, 4)
        e.wait_ge(tail_s, 1)
        for c in range(NCH):
            w = width(c)
            for name, dst, src, free in (("B2", B2, b, ("pe", "Bt")), ("K2", K2, kd, ("pe", "Kt")), ("A2", A2, a, ("pe", "Y")),
                                         ("V2", V2, v, ("pe", "X3"))):
                for g in range(GROUPS):
                    after(e, *free, c - 1, g)
                    if c:
                        after(e, "pe", "Vt", c - 1, g)
                    if name == "V2" and c:
                        after(e, "pe", "XT4", c - 1, g)
                    if c == last:
                        for h in range(2):
                            rows = slice(h * HD, (h + 1) * HD)
                            e.memset(dst[rows, g * G:(g + 1) * G, h * CH + WL:(h + 1) * CH], 0.0)
                    done("pool", blocks(e, e.tensor_copy, dst, src[:, g * G:(g + 1) * G, c * CH:c * CH + w], g, w))

    k.n_zero = 4
    k.rw_done = {"sems": sems, "value": value}
    return Stage(pe, act, dve, pool)


def stage_rwkv_out(k):
    hw = TOK // 2
    y, yb, mg = k.rw_s, k.rw_y, k.rw_mg
    last = NCH - 1
    k.psum.add("rw_mean", ["act", "act"] * KT)
    plan_product(k, "rw_g2", k.A["rw_g2_2"][0], [(0, D)], "dve")
    plan_product(k, "rw_o", k.A["rw_wo_2"][0], [(0, D)], "dve")
    B = k.psum.base
    k.hold[k.weights.base["rw_g2"]] = (k.rw_done["sems"]["act"], k.rw_done["value"]("act", "Y", last, GROUPS - 1))
    d_s, sq_s = k.sem("gn_centred"), k.sem("gn_square")
    mean = k.rw_r
    rs = k.rw_k

    def pe(e):
        e.wait_ge(k.rw_done["sems"]["act"], k.rw_done["value"]("act", "Y", last, GROUPS - 1))
        e.wait_ge(k.rw_done["sems"]["dve"], k.rw_done["value"]("dve", "U", last, GROUPS - 1))

        def total(g, src, f):
            take(e, k, g)
            for h in range(2):
                mm = e.matmul(k.pp[g % NB][:, h, 0:hw], k.pair[:, :], src[:, f, h * hw:(h + 1) * hw], start=True, stop=True)
            mm.then_inc(k.full, 1)

        for f in range(KT + 1):
            if f < KT:
                total(B["rw_mean"] + (2 * f if f == 0 else 2 * f - 1), y, f)
            if f:
                e.wait_ge(sq_s, f)
                total(B["rw_mean"] + (2 * f if f < KT else 2 * f - 1), k.rw_v, f - 1)
        product(e, k, "rw_g2", lambda kt, h: mg[0:(P, 32)[kt], kt, h * hw:(h + 1) * hw], lambda kt: None)
        product(e, k, "rw_o", lambda kt, h: y[:, kt, h * hw:(h + 1) * hw], lambda kt: was_read(e, k, B["rw_g2"] + kt))

    def g_mean(f):
        return B["rw_mean"] + (0 if f == 0 else 2 * f - 1)

    def g_var(f):
        return B["rw_mean"] + (2 * f + 2 if f < KT - 1 else 2 * f + 1)

    def act(e):
        e.wait_ge(k.rw_done["sems"]["act"], k.rw_done["value"]("act", "Y", last, GROUPS - 1))
        for f in range(KT + 1):
            if f < KT:
                g = g_mean(f)
                filled(e, k, g)
                freed(k, g, e.activation(halves(mean[:, f, :]), k.pp[g % NB][:, :, 0:hw], ACT.Copy, scale=1.0 / HD))
                e.wait_ge(d_s, f + 1)
                e.activation(k.rw_v[:, f, :], y[:, f, :], ACT.Square).then_inc(sq_s, 1)
            if f:
                g = g_var(f - 1)
                filled(e, k, g)
                freed(k, g, e.activation(halves(rs[:, f - 1, :]), k.pp[g % NB][:, :, 0:hw], ACT.Sqrt, bias=k.small[:, 41:42],
                                         scale=1.0 / HD))

    def dve(e):
        for f in range(KT + 1):
            if f < KT:
                was_read(e, k, g_mean(f))
                e.tensor_tensor(y[:, f, :], y[:, f, :], mean[:, f, :], ALU.subtract).then_inc(d_s, 1)
            if f:
                was_read(e, k, g_var(f - 1))
                f -= 1
                link(e, k, e.reciprocal(rs[:, f, :], rs[:, f, :]))
                e.wait_ge(sq_s, f + 1)
                link(e, k, e.scalar_tensor_tensor(y[:, f, :], y[:, f, :], pcol(k, "rw_lnx_g", f), rs[:, f, :], ALU.mult, ALU.mult))
                link(e, k, e.scalar_tensor_tensor(y[:, f, :], y[:, f, :], pcol(k, "rw_lnx_b", f), yb[:, f, :], ALU.add, ALU.add))
        for f in range(KT):
            g = B["rw_g2"] + f
            filled(e, k, g)
            freed(k, g, e.tensor_tensor(halves(y[:, f, :]), k.pp[g % NB][:, :, 0:hw], halves(y[:, f, :]), ALU.mult))
            was_read(e, k, g)
        add(e)

    add = residual(k, "rw_o", 0)
    return Stage(pe, act, dve)


def stage_ffn(k, l):
    hw = TOK // 2
    hb = k.h_base
    NF = FF2 // P
    NU = FF2 // GW
    up, down = f"ffn_up{l}", f"ffn_down{l}"
    cols = []
    for u in range(NU):
        cols += [(u * GW, (u + 1) * GW), (FF2 + u * GW, FF2 + (u + 1) * GW)]
    plan_product(k, up, k.A["ffn_up_2"][l], cols, "act")
    plan_product(k, down, k.A["ffn_down_2"][l], [(0, D)], "dve")
    g0 = k.psum.base[up]
    at = 0
    hid = k.work(at, NF, TOK); at += NF * TOK
    R = 8
    ub = k.work(at, R, TOK + 2); at += R * (TOK + 2)
    cv = k.work(at, R, TOK); at += R * TOK
    pad, conv, silu, hid_s = (k.sem(f"ffn{l}_" + n) for n in ("pad", "conv_ready", "silu_ready", "hidden_ready"))
    before = list(k.x_before)

    def channel(n):
        return 2 * (n // 4) + n % 2 + (NF if n % 4 >= 2 else 0)

    def pe(e):
        product(e, k, up, h_tile(k, 0), h_wait(e, k, hb))
        product(e, k, down, lambda kt, h: hid[:, kt, h * hw:(h + 1) * hw], lambda kt: e.wait_ge(hid_s, kt + 1))

    def act(e):
        def gate(n):
            e.wait_ge(conv, n + 1)
            e.activation(cv[:, n % R, :], cv[:, n % R, :], ACT.Silu).then_inc(silu, 1)

        e.wait_ge(pad, 1)
        for n in range(2 * NF):
            filled(e, k, g0 + n)
            if n >= R:
                e.wait_ge(conv, n - R + 1)
            freed(k, g0 + n, e.copy(halves(ub[:, n % R, 2:TOK + 2]), k.pp[(g0 + n) % NB][:, :, 0:hw]))
            if n >= 2 and (n - 2) % 4 < 2:
                gate(n - 2)

    def dve(e):
        for n in range(2 * NF):
            was_read(e, k, g0 + n)
            if n >= R:
                e.wait_ge(hid_s, 2 * ((n - R) // 4) + n % 2 + 1)
            f = channel(n)
            o = cv[:, n % R, :]
            link(e, k, e.tensor_scalar(o, ub[:, n % R, 0:TOK], pcol(k, f"ffn_w{l}0", f), pcol(k, f"ffn_b{l}", f), ALU.mult, ALU.add))
            link(e, k, e.scalar_tensor_tensor(o, ub[:, n % R, 1:TOK + 1], pcol(k, f"ffn_w{l}1", f), o, ALU.mult, ALU.add))
            e.scalar_tensor_tensor(o, ub[:, n % R, 2:TOK + 2], pcol(k, f"ffn_w{l}2", f), o, ALU.mult, ALU.add).then_inc(conv, 1)
        add(e)

    def pool(e):
        for g in before:
            was_read(e, k, g)
        e.memset(ub[:, :, 0:2], 0.0).then_inc(pad, 1)
        for f in range(NF):
            e.wait_ge(silu, f + 1)
            n = 4 * (f // 2) + f % 2
            e.wait_ge(conv, n + 3)
            e.tensor_tensor(hid[:, f, :], cv[:, n % R, :], cv[:, (n + 2) % R, :], ALU.mult).then_inc(hid_s, 1)

    add = residual(k, down, 0)
    return Stage(pe, act, dve, pool)


def stage_stick(k):
    hw = TOK // 2
    hb = k.h_base
    A = k.A
    spans = [(0, META)] + [(META + t * P, META + (t + 1) * P) for t in range(4)]
    plan_product(k, "sb_q", A["sb_wq_2"][0], [(0, D)], "act")
    plan_product(k, "sb_k", A["sb_wk_2"], [(0, D)], "act")
    plan_tokens(k, "sb_v", A["sb_wv_2"], (0, D), spans, ["act", "dve", "dve"])
    last_tile = len(k.psum.readers)
    plan_product(k, "sb_out", A["sb_wo_2"][0], [(0, D)], "dve")
    B = k.psum.base
    kvn = k.kvn
    at = KT * TOK
    q = k.work(at, KT, 2, TOK); at += KT * 2 * TOK
    kT = k.work(at, KT, TOK); at += KT * TOK
    v = k.work(at, 5, D); at += 5 * D
    o = k.work(at, KT, TOK); at += KT * TOK
    az, sp, inc = k.h[:, 0:3, 0:TOK], k.h[:, 3:5, 0:TOK], k.h[:, 5:8, 0:TOK]
    w = k.work(0, 3, TOK)
    wT = k.work(3 * TOK, 3, 5 * P)
    S = [k.pp[i].rearrange("p a b -> p (a b)") for i in range(2)]
    zero = k.sem("sb_zeroed")
    z_s, abs_s, ln_s, t_s, w_s, turn_s, wt_s, o_full, o_s = (k.sem("sb_" + n) for n in (
        "scores", "abs", "ln_ready", "log_weight_ready", "weight_ready", "turned", "turned_ready", "o_full", "o_read"))
    steps = [(h, i) for h in range(HEADS) for i in range(5)]
    N = len(steps)
    before = list(k.x_before)
    OFF = 512 - META

    def dims(n):
        h, i = steps[n]
        a, b = spans[i]
        return h, i, a, b, b - a

    def pe(e):
        product(e, k, "sb_q", h_tile(k, 0), h_wait(e, k, hb))
        product(e, k, "sb_k", h_tile(k, 0, kvn), h_wait(e, k, hb + KT))
        product_tokens(e, k, "sb_v", lambda kt, a, b: kvn[:, kt, a:b], lambda kt: None)
        for g in range(last_tile - NB, last_tile):
            was_read(e, k, g)

        def scores(n):
            h, i, a, b, m = dims(n)
            if n >= 2:
                e.wait_ge(t_s, n - 1)
            z = S[n % 2][0:m]
            qt = q[:, h // 2, h % 2, a:b]
            mm = e.matmul(z[:, OFF:512], qt, kT[:, h // 2, 0:META], start=True, stop=i > 0)
            if i > 0:
                e.matmul(z[:, 512:OFF + b], qt, kT[:, h // 2, META:b], start=True, stop=False)
            e.matmul(z[:, OFF + a:OFF + b], k.ident[0:m, 0:m], k.mask_lt[0:m, 0:m], start=False, stop=True).then_inc(z_s, 1)

        def turn(n):
            h, i, a, b, m = dims(n)
            e.wait_ge(w_s, n + 1)
            if n >= 2:
                e.wait_ge(o_s, n - 1)
                e.wait_ge(wt_s, n - 1)
            mm = e.transpose(k.bank[6 + n % 2][0:META, P:P + m], w[0:m, n % 3, 0:META], k.ident[0:m, 0:m])
            for j in range(1, i + 1):
                mm = e.transpose(k.bank[4 + n % 2][:, (j - 1) * P:(j - 1) * P + m], w[0:m, n % 3, META + (j - 1) * P:META + j * P],
                                 k.ident[0:m, 0:m])
            mm.then_inc(turn_s, 1)

        def values(n):
            h, i, a, b, m = dims(n)
            e.wait_ge(wt_s, n + 1)
            r = h % 2 * HD
            for j in range(i + 1):
                kj = META if j == 0 else P
                mm = e.matmul(k.bank[6 + n % 2][r:r + HD, 0:m], v[0:kj, j, h * HD:(h + 1) * HD],
                              wT[0:kj, n % 3, j * P:j * P + m], start=j == 0, stop=j == i)
            mm.then_inc(o_full, 1)

        for n in range(N + 3):
            if n < N:
                scores(n)
            if 0 <= n - 2 < N:
                turn(n - 2)
            if 0 <= n - 3 < N:
                values(n - 3)
        product(e, k, "sb_out", lambda kt, h: o[:, kt, h * hw:(h + 1) * hw], lambda kt: e.wait_ge(o_s, 10 * (kt + 1)))

    def act(e):
        e.wait_ge(zero, 1)
        for f in range(KT):
            g = B["sb_q"] + f
            filled(e, k, g)
            for h in range(2):
                rows = slice(h * HD, (h + 1) * HD)
                op = e.activation(halves(q[rows, f, h, :]), k.pp[g % NB][rows, :, 0:hw], ACT.Copy, scale=HD ** -0.5)
            freed(k, g, op)
        for f in range(KT):
            g = B["sb_k"] + f
            filled(e, k, g)
            freed(k, g, e.copy(halves(kT[:, f, :]), k.pp[g % NB][:, :, 0:hw]))
        read_tokens(k, "sb_v", e, "act", v)

        def soft(n):
            h, i, a, b, m = dims(n)
            e.wait_ge(z_s, n + 1)
            if n >= 3:
                e.wait_ge(w_s, n - 2)
            t = az[0:m, n % 3, 0:b]
            e.activation(t, S[n % 2][0:m, OFF:OFF + b], ACT.Abs).then_inc(abs_s, 1)
            e.wait_ge(abs_s, 2 * n + 1)
            e.activation(t, t, ACT.Exp, scale=-1.0).then_inc(abs_s, 1)
            e.wait_ge(abs_s, 2 * n + 2)
            e.activation(t, t, ACT.Ln, bias=1.0).then_inc(ln_s, 1)

        def weight(n):
            h, i, a, b, m = dims(n)
            e.wait_ge(t_s, n + 1)
            if n >= 3:
                e.wait_ge(turn_s, n - 2)
            e.activation(w[0:m, n % 3, 0:b], az[0:m, n % 3, 0:b], ACT.Exp).then_inc(w_s, 1)

        def copies(n):
            h, i, a, b, m = dims(n)
            e.wait_ge(turn_s, n + 1)
            if n >= 3:
                e.wait_ge(o_full, n - 2)
            if i:
                src = k.bank[4 + n % 2][:, 0:i * P].rearrange("p (j n) -> p j n", n=P)
                e.copy(wT[:, n % 3, P:(i + 1) * P].rearrange("p (j n) -> p j n", n=P)[:, :, 0:m], src[:, :, 0:m])
            e.copy(wT[0:META, n % 3, 0:m], k.bank[6 + n % 2][0:META, P:P + m]).then_inc(wt_s, 1)

        e.preload_act_table_set("natural_log_exp_and_others")
        e.wait_ge(k.full, last_tile)
        for n in range(N + 2):
            if n < N:
                soft(n)
            if 0 <= n - 1 < N:
                weight(n - 1)
            if 0 <= n - 2 < N:
                copies(n - 2)

    def dve(e):
        read_tokens(k, "sb_v", e, "dve", v)

        def logs(n):
            h, i, a, b, m = dims(n)
            e.wait_ge(ln_s, n + 1)
            t, s_, c = az[0:m, n % 3, 0:b], sp[0:m, n % 2, 0:b], inc[0:m, n % 3, 0:b]
            z = S[n % 2][0:m, OFF:OFF + b]
            link(e, k, e.scalar_tensor_tensor(s_, z, 0.0, t, ALU.max, ALU.add))
            link(e, k, e.tensor_tensor_scan(c[:, ::-1], k.ones[0:m, 0:1].to_broadcast([m, b]), s_[:, ::-1], 0.0, ALU.mult, ALU.add))
            e.tensor_tensor(t, z, c, ALU.subtract).then_inc(t_s, 1)

        def outs(n):
            h, i, a, b, m = dims(n)
            e.wait_ge(o_full, n + 1)
            r = h % 2 * HD
            e.tensor_copy(o[r:r + HD, h // 2, a:b], k.bank[6 + n % 2][r:r + HD, 0:m]).then_inc(o_s, 1)

        for n in range(N + 3):
            if n < N:
                logs(n)
            if 0 <= n - 3 < N:
                outs(n - 3)
        add(e)

    def pool(e):
        for g in before:
            was_read(e, k, g)
        e.memset(q, 0.0).then_inc(zero, 1)

    add = residual(k, "sb_out", 0)
    return Stage(pe, act, dve, pool)


def stage_store(k):
    k.psum.add("out", ["dve", "act"] * 2)
    g = k.psum.base["out"]
    src = list(k.x_ready)
    hb = k.h_base
    orow = k.work(0, 4, D)
    fin = STOP is None

    def pe(e):
        for t in range(4):
            take(e, k, g + t)
            for f in range(KT):
                if fin:
                    e.wait_ge(k.h_ready, hb + f + 1)
                    s = k.h[:, f, 1 + META + t * P:1 + META + (t + 1) * P]
                else:
                    was_read(e, k, src[f])
                    s = k.x[:, f, META + t * P:META + (t + 1) * P]
                mm = e.transpose(k.pp[(g + t) % NB][:, f // 4, (f % 4) * P:(f % 4 + 1) * P], s, k.ident[:, :])
            mm.then_inc(k.full, 1)

    def dve(e):
        for t in range(0, 4, 2):
            filled(e, k, g + t)
            freed(k, g + t, e.tensor_copy(halves(orow[:, t, :]), k.pp[(g + t) % NB][:, :, :]))

    def act(e):
        for t in range(1, 4, 2):
            filled(e, k, g + t)
            freed(k, g + t, e.copy(halves(orow[:, t, :]), k.pp[(g + t) % NB][:, :, :]))

    def sync(e):
        for t in range(4):
            was_read(e, k, g + t)
            e.dma_start(k.out[0, t * P:(t + 1) * P, :], orow[:, t, :]).then_inc(k.stored, 16)
        e.wait_ge(k.stored, 64)

    return Stage(pe, act, dve, sync=sync)


def mark(k):
    k.rw_tiles = len(k.psum.readers)


def plan(k):
    k.n_norm = k.n_h = 0
    k.hold = {}
    plan_params(k)
    at = 0
    k.xb = k.work(at, KT, SEQ + 4); at += KT * (SEQ + 4)
    k.xc = k.work(at, KT, SEQ); at += KT * SEQ
    k.lr = k.work(at, KT, SEQ); at += KT * SEQ
    k.li = k.work(at, KT, SEQ); at += KT * SEQ
    k.lT = k.work(at, KT, SEQ); at += KT * SEQ
    k.lgate = k.work(at, KT, SEQ); at += KT * SEQ
    k.ld = k.work(at, SEQ); at += SEQ
    k.wri = k.work(at, 2, KT, P); at += 2 * KT * P
    k.prow = k.work(at, 5, P); at += 5 * P
    k.mrow = k.lr.rearrange("p a b -> p (a b)")[:, 0:D]
    k.xrow = k.lT.rearrange("p a b -> p (a b)").rearrange("p (t n) -> p t n", t=4)
    k.wri_loaded = k.sem("wri_loaded")

    st = [stage_turn_inputs(k)]

    def upto(name, *make):
        if k.stopped:
            return
        for m in make:
            st.append(m())
        k.stopped = STOP == name

    k.stopped = False
    upto("lru", lambda: stage_norm(k, ["mix_norm0"], META), lambda: stage_lru(k))
    upto("mlp0", lambda: stage_norm(k, ["mlp_norm0"], META), lambda: stage_mlp(k, 0))
    upto("fox", lambda: stage_norm(k, ["mix_norm1"], META), lambda: stage_fox(k))
    upto("mlp1", lambda: stage_norm(k, ["mlp_norm1"], META), lambda: stage_mlp(k, 1))
    upto("rwkv", lambda: stage_norm(k, ["norm_mix0"], 0), lambda: stage_rwkv_project(k),
         lambda: mark(k) or stage_rwkv_chunks(k), lambda: stage_rwkv_out(k))
    upto("ffn0", lambda: stage_norm(k, ["norm_ffn0"], 0), lambda: stage_ffn(k, 0))
    k.kvn = k.work(0, KT, TOK)
    upto("sb", lambda: stage_norm(k, ["norm_mix1", "kv_norm"], 0, [k.h[:, :, 1:TOK + 1], k.kvn]), lambda: stage_stick(k))
    upto("ffn1", lambda: stage_norm(k, ["norm_ffn1"], 0), lambda: stage_ffn(k, 1))
    if STOP is None:
        st.append(stage_norm(k, ["final_norm"], 0))
    st.append(stage_store(k))
    return st


_INS = [
    "x", "mix_norm", "mlp_norm", "mlp_w1", "mlp_w2", "lru_w_in", "lru_conv_w", "lru_conv_b", "lru_w_r", "lru_b_r",
    "lru_w_i", "lru_b_i", "lru_lambda", "lru_w_out", "fox_w_in", "fox_b_f", "fox_q_gain", "fox_k_gain", "fox_w_out",
    "meta_tokens_2", "norm_mix_g_2", "norm_ffn_g_2", "ffn_up_2", "ffn_conv_w_2", "ffn_conv_b_2", "ffn_down_2",
    "rw_mix_2", "rw_wr_2", "rw_wk_2", "rw_wv_2", "rw_wo_2", "rw_w0_2", "rw_w1_2", "rw_w2_2", "rw_a0_2", "rw_a1_2",
    "rw_a2_2", "rw_g1_2", "rw_g2_2", "rw_kk_2", "rw_ka_2", "rw_rk_2", "rw_lnx_g_2", "rw_lnx_b_2", "kv_norm_g_2",
    "sb_wk_2", "sb_wv_2", "sb_wq_2", "sb_wo_2", "final_norm_g_2",
]


def kernel(**inputs):
    import numpy as _np
    import concourse.bacc as _bacc
    from concourse import mybir as _mybir
    from concourse.bass_utils import run_bass_kernel_spmd as _run

    nc = _bacc.Bacc("TRN2", target_bir_lowering=False, num_devices=1)
    arrays, args = {}, {}
    for name in _INS:
        a = _np.ascontiguousarray(inputs[name])
        arrays[f"in_{name}_dram"] = a
        args[name] = nc.dram_tensor(f"in_{name}_dram", a.shape, _mybir.dt.from_np(a.dtype), kind="ExternalInput").ap()
    out = nc.dram_tensor("out_0_dram", (1, SEQ, D), F32, kind="ExternalOutput").ap()
    build(nc, args, out)
    r = _run(nc, [arrays], core_ids=[0])
    return r.results[0]["out_0_dram"]
```
